# Optimizing a Trainium2 kernel written in Bass

```python
import jax, jax.numpy as jnp
from jax import lax
import numpy as np
import math

D_MODEL = 1024
BATCH = 1
SEQ = 512
DEPTH = 2

N_A_LAYERS = DEPTH // 2
N_B_LAYERS = DEPTH - N_A_LAYERS

D_FF = ((8 * D_MODEL // 3 + 255) // 256) * 256
N_FFN_PER_LAYER = 2

POOL_WINDOWS = (2, 4, 8, 16)
POOL_GROUPS = len(POOL_WINDOWS)
POOL_GROUP_DIM = D_MODEL // POOL_GROUPS

ATTN_GROUPS = ((128, 1), (512, 4), (2048, 16))
N_ATTN_GROUPS = len(ATTN_GROUPS)
HEAD_DIM = 64
HEADS_PER_GROUP = D_MODEL // (2 * HEAD_DIM)
QKV_WIDTH = N_ATTN_GROUPS * HEADS_PER_GROUP * HEAD_DIM
O_WIDTH = HEADS_PER_GROUP * HEAD_DIM
ROPE_THETA = 10000.0

N_NORMS_PER_LAYER = 6
RMS_EPS = 1e-6
NEG_BIG = -1e30


def rms_norm(x, gain):
    x32 = x.astype(jnp.float32)
    y = x32 * lax.rsqrt(jnp.mean(x32 * x32, axis=-1, keepdims=True) + RMS_EPS) * gain.astype(jnp.float32)
    return y.astype(x.dtype)

def swiglu(h, w_gate, w_up, w_down):
    return (jax.nn.silu(h @ w_gate) * (h @ w_up)) @ w_down

def rope_tables(positions):
    inv_freq = ROPE_THETA ** (-jnp.arange(0, HEAD_DIM, 2, dtype=jnp.float32) / HEAD_DIM)
    ang = positions.astype(jnp.float32)[..., None] * inv_freq
    return jnp.cos(ang), jnp.sin(ang)

def apply_rope(x, cos, sin):
    extra = x.ndim - 3
    shape = cos.shape[:2] + (1,) * extra + cos.shape[-1:]
    c = cos.reshape(shape)
    s = sin.reshape(shape)
    x32 = x.astype(jnp.float32)
    x1, x2 = jnp.split(x32, 2, axis=-1)
    out = jnp.concatenate([x1 * c - x2 * s, x2 * c + x1 * s], axis=-1)
    return out.astype(x.dtype)

def pool_mixer(h, w_in, w_group, scale, w_out):
    B, S, _ = h.shape
    u = h @ w_in
    u32 = u.astype(jnp.float32)
    csum = jnp.cumsum(u32, axis=1)
    t = jnp.arange(S)
    pooled = []
    for g, w in enumerate(POOL_WINDOWS):
        lo, hi = g * POOL_GROUP_DIM, (g + 1) * POOL_GROUP_DIM
        c = csum[..., lo:hi]
        c_prev = jnp.pad(c, ((0, 0), (w, 0), (0, 0)))[:, :S]
        count = jnp.minimum(t + 1, w).astype(jnp.float32)[None, :, None]
        pooled.append((c - c_prev) / count - u32[..., lo:hi])
    p = jnp.stack(pooled, axis=2).astype(u.dtype)
    y = jnp.einsum('bsgc,gcd->bsgd', p, w_group).reshape(B, S, D_MODEL) * scale
    return y @ w_out

def dilated_window_attention(q, k, v, window, dilation):
    B, S, H, Dh = q.shape
    blk = window // dilation
    span = blk * dilation
    s_pad = -(-S // span) * span
    nb = s_pad // span

    def split(a):
        a = jnp.pad(a, ((0, 0), (0, s_pad - S), (0, 0), (0, 0)))
        return a.reshape(B, nb, blk, dilation, H, Dh)

    def with_prev(a):
        prev = jnp.pad(a[:, :-1], ((0, 0), (1, 0), (0, 0), (0, 0), (0, 0), (0, 0)))
        return jnp.concatenate([prev, a], axis=2)

    qb = split(q)
    kc = with_prev(split(k))
    vc = with_prev(split(v))
    s = jnp.einsum('bnqrhd,bnkrhd->bnrhqk', qb, kc, preferred_element_type=jnp.float32) * (Dh ** -0.5)
    qi = jnp.arange(blk)[:, None]
    kj = jnp.arange(2 * blk)[None, :]
    band = (kj >= qi) & (kj <= qi + blk)
    valid_prev = (jnp.arange(nb)[:, None, None] > 0) | (kj[None] >= blk)
    mask = band[None] & valid_prev
    s = jnp.where(mask[None, :, None, None], s, NEG_BIG)
    m = jnp.max(s, axis=-1, keepdims=True)
    p = jnp.exp(s - m)
    den = jnp.sum(p, axis=-1, keepdims=True)
    o = jnp.einsum('bnrhqk,bnkrhd->bnqrhd', (p / den).astype(v.dtype), vc)
    lse = (m + jnp.log(den))[..., 0]
    o = o.reshape(B, s_pad, H, Dh)[:, :S]
    lse = lse.transpose(0, 1, 4, 2, 3).reshape(B, s_pad, H)[:, :S]
    return o, lse

def shared_kv(h, kv_gain, w_k, w_v, cos, sin):
    B, S, _ = h.shape
    hk = rms_norm(h, kv_gain)
    k = (hk @ w_k).reshape(B, S, N_ATTN_GROUPS, HEADS_PER_GROUP, HEAD_DIM)
    v = (hk @ w_v).reshape(B, S, N_ATTN_GROUPS, HEADS_PER_GROUP, HEAD_DIM)
    return apply_rope(k, cos, sin), v

def dilated_mixer(h, cos, sin, w_q, k_sh, v_sh, w_o):
    B, S, _ = h.shape
    q = (h @ w_q).reshape(B, S, N_ATTN_GROUPS, HEADS_PER_GROUP, HEAD_DIM)
    q = apply_rope(q, cos, sin)
    outs, lses = [], []
    for g, (window, dilation) in enumerate(ATTN_GROUPS):
        o, l = dilated_window_attention(q[:, :, g], k_sh[:, :, g], v_sh[:, :, g], window, dilation)
        outs.append(o)
        lses.append(l)
    wts = jax.nn.softmax(jnp.stack(lses, axis=0), axis=0)
    o = jnp.sum(wts[..., None] * jnp.stack(outs, axis=0).astype(jnp.float32), axis=0).astype(h.dtype)
    return o.reshape(B, S, O_WIDTH) @ w_o

def first_inputs(seed: int = 0) -> dict:
    key = jax.random.key(seed)
    ks = jax.random.split(key, 16)
    f32 = jnp.float32

    def w(k, shape, fan_in):
        return jax.random.normal(k, shape, f32) * (fan_in ** -0.5)

    x = jax.random.normal(ks[0], (BATCH, SEQ, D_MODEL), f32)
    offset = jax.random.randint(ks[1], (BATCH, 1), 0, 1024, dtype=jnp.int32)
    positions = (jnp.arange(SEQ, dtype=jnp.int32)[None, :] + offset).astype(jnp.int32)
    norm_gain = 1.0 + 0.05 * jax.random.normal(ks[2], (DEPTH, N_NORMS_PER_LAYER, D_MODEL), f32)
    ffn_w_gate = w(ks[3], (DEPTH, N_FFN_PER_LAYER, D_MODEL, D_FF), D_MODEL)
    ffn_w_up = w(ks[4], (DEPTH, N_FFN_PER_LAYER, D_MODEL, D_FF), D_MODEL)
    ffn_w_down = w(ks[5], (DEPTH, N_FFN_PER_LAYER, D_FF, D_MODEL), D_FF)
    pool_w_in = w(ks[6], (N_A_LAYERS, D_MODEL, D_MODEL), D_MODEL)
    pool_w_group = w(ks[7], (N_A_LAYERS, POOL_GROUPS, POOL_GROUP_DIM, POOL_GROUP_DIM), POOL_GROUP_DIM)
    pool_scale = 1.0 + 0.1 * jax.random.normal(ks[8], (N_A_LAYERS, D_MODEL), f32)
    pool_w_out = w(ks[9], (N_A_LAYERS, D_MODEL, D_MODEL), D_MODEL)
    kv_norm_gain = 1.0 + 0.05 * jax.random.normal(ks[10], (D_MODEL,), f32)
    w_k = w(ks[11], (D_MODEL, QKV_WIDTH), D_MODEL)
    w_v = w(ks[12], (D_MODEL, QKV_WIDTH), D_MODEL)
    attn_w_q = w(ks[13], (N_B_LAYERS, D_MODEL, QKV_WIDTH), D_MODEL)
    attn_w_o = w(ks[14], (N_B_LAYERS, O_WIDTH, D_MODEL), O_WIDTH)
    return {
        "x": x, "positions": positions, "norm_gain": norm_gain,
        "ffn_w_gate": ffn_w_gate, "ffn_w_up": ffn_w_up, "ffn_w_down": ffn_w_down,
        "pool_w_in": pool_w_in, "pool_w_group": pool_w_group, "pool_scale": pool_scale,
        "pool_w_out": pool_w_out, "kv_norm_gain": kv_norm_gain, "w_k": w_k, "w_v": w_v,
        "attn_w_q": attn_w_q, "attn_w_o": attn_w_o,
    }

def first_block(x, positions, norm_gain, ffn_w_gate, ffn_w_up, ffn_w_down, pool_w_in, pool_w_group,
              pool_scale, pool_w_out, kv_norm_gain, w_k, w_v, attn_w_q, attn_w_o):
    cos, sin = rope_tables(positions)
    h = x
    k_sh = None
    v_sh = None
    for layer in range(DEPTH):
        g = norm_gain[layer]
        f = swiglu(rms_norm(h, g[0]), ffn_w_gate[layer, 0], ffn_w_up[layer, 0], ffn_w_down[layer, 0])
        h = h + 0.5 * rms_norm(f, g[1])
        hm = rms_norm(h, g[2])
        if layer < N_A_LAYERS:
            mix = pool_mixer(hm, pool_w_in[layer], pool_w_group[layer], pool_scale[layer], pool_w_out[layer])
        else:
            b = layer - N_A_LAYERS
            mix = dilated_mixer(hm, cos, sin, attn_w_q[b], k_sh, v_sh, attn_w_o[b])
        h = h + rms_norm(mix, g[3])
        f = swiglu(rms_norm(h, g[4]), ffn_w_gate[layer, 1], ffn_w_up[layer, 1], ffn_w_down[layer, 1])
        h = h + 0.5 * rms_norm(f, g[5])
        if layer == N_A_LAYERS - 1:
            k_sh, v_sh = shared_kv(h, kv_norm_gain, w_k, w_v, cos, sin)
    return h


CTX_LEN = 256
GRID_W = 64
N_MIXERS = 4
GROUP_W = D_MODEL // N_MIXERS
D_MIX = GROUP_W * N_MIXERS
HG_DK = 64
HG_DV = 64
HG_HEADS = GROUP_W // HG_DV
HG_CHUNK = 64
GA_HEADS = GROUP_W // HEAD_DIM
GA_KV = GA_HEADS // 2
DF_V = 64
DF_QK = DF_V // 2
DF_HEADS = GROUP_W // DF_V
WN_HEADS = GROUP_W // HEAD_DIM
WN_KV = WN_HEADS // 2
WINDOW = 128
Q_BLOCK = 128
LN_EPS = 1e-5

IN_WIDTHS = (
    HG_HEADS * HG_DK, HG_HEADS * HG_DV, HG_HEADS * HG_DK, HG_HEADS * HG_DK,
    GA_HEADS * HEAD_DIM, GA_KV * HEAD_DIM, GA_KV * HEAD_DIM,
    DF_HEADS * 2 * DF_QK, DF_HEADS * 2 * DF_QK, DF_HEADS * DF_V,
    WN_HEADS * HEAD_DIM, WN_KV * HEAD_DIM, WN_KV * HEAD_DIM,
    D_MIX,
)
IN_WIDTH = sum(IN_WIDTHS)
SPLIT_AT = tuple(int(v) for v in np.cumsum(IN_WIDTHS)[:-1])


def rms_norm_2(x, g):
    xf = x.astype(jnp.float32)
    y = xf * lax.rsqrt(jnp.mean(xf * xf, axis=-1, keepdims=True) + RMS_EPS)
    return (y * g).astype(x.dtype)

def layer_norm(x, g, b):
    xf = x.astype(jnp.float32)
    mu = jnp.mean(xf, axis=-1, keepdims=True)
    var = jnp.mean(jnp.square(xf - mu), axis=-1, keepdims=True)
    return ((xf - mu) * lax.rsqrt(var + LN_EPS) * g + b).astype(x.dtype)

def split_heads(t, n_heads):
    return t.reshape(t.shape[:-1] + (n_heads, t.shape[-1] // n_heads))

def merge_heads(t):
    return t.reshape(t.shape[:2] + (-1,))

def axial_rope(n_tok, dim):
    rows = n_tok // GRID_W
    row = jnp.repeat(jnp.arange(rows, dtype=jnp.float32), GRID_W)
    col = jnp.broadcast_to(jnp.arange(GRID_W, dtype=jnp.float32), (rows, GRID_W)).reshape(-1)
    d_axis = dim // 2
    inv = ROPE_THETA ** (-jnp.arange(0, d_axis, 2, dtype=jnp.float32) / d_axis)
    ang_r = row[:, None] * inv
    ang_c = col[:, None] * inv
    ang = jnp.concatenate([ang_r, ang_r, ang_c, ang_c], axis=-1)
    return jnp.cos(ang), jnp.sin(ang)

def apply_rope_2(x, rope):
    cos, sin = rope
    a1, a2, b1, b2 = jnp.split(x, 4, axis=-1)
    rot = jnp.concatenate([-a2, a1, -b2, b1], axis=-1)
    return (x * cos[:, None, :] + rot * sin[:, None, :]).astype(x.dtype)

def sweep_query_blocks(fn, q):
    b, s = q.shape[0], q.shape[1]
    nb = s // Q_BLOCK
    qb = jnp.moveaxis(q.reshape((b, nb, Q_BLOCK) + q.shape[2:]), 1, 0)
    out = lax.map(fn, qb)
    return jnp.moveaxis(out, 0, 1).reshape((b, s) + out.shape[3:])

def hgrn_forget(z, lb):
    f = lb + (1.0 - lb) * jax.nn.sigmoid(z.astype(jnp.float32))
    return (1.0 - f).astype(z.dtype), jnp.log(f)

def gla_chunk_scan(q, k, v, logf, s0):
    b, t, h, _ = q.shape
    dv = v.shape[-1]
    nc = t // HG_CHUNK

    def to_chunks(a):
        return jnp.moveaxis(a.reshape(b, nc, HG_CHUNK, h, a.shape[-1]), 1, 0)

    incl = jnp.tril(jnp.ones((HG_CHUNK, HG_CHUNK), dtype=bool))

    def step(s, xs):
        qc, kc, vc, fc = xs
        qf, kf, vf = qc.astype(jnp.float32), kc.astype(jnp.float32), vc.astype(jnp.float32)
        bcum = jnp.cumsum(fc, axis=1)
        o_inter = jnp.einsum('bthk,bhkv->bthv', qf * jnp.exp(bcum), s)
        diff = bcum[:, :, None] - bcum[:, None, :]
        decay = jnp.exp(jnp.where(incl[None, :, :, None, None], diff, -jnp.inf))
        att = jnp.einsum('bthk,bshk,btshk->bhts', qf, kf, decay)
        o_intra = jnp.einsum('bhts,bshv->bthv', att, vf)
        blast = bcum[:, -1]
        s_new = jnp.exp(blast)[..., None] * s + jnp.einsum(
            'bshk,bshv->bhkv', kf * jnp.exp(blast[:, None] - bcum), vf)
        return s_new, (o_inter + o_intra).astype(v.dtype)

    s_fin, o = lax.scan(step, s0, (to_chunks(q), to_chunks(k), to_chunks(v), to_chunks(logf)))
    return jnp.moveaxis(o, 0, 1).reshape(b, t, h, dv), s_fin

def gla_final_state(k, v, logf):
    after = lax.cumsum(logf, axis=1, reverse=True) - logf
    return jnp.einsum('bshk,bshv->bhkv', k.astype(jnp.float32) * jnp.exp(after), v.astype(jnp.float32))

def hgrn2_mixer(q, i, f_fwd, f_bwd, qc, ic, fc_fwd, fc_bwd, lb, norm_g, ctx_out):
    hs = lambda t: split_heads(t, HG_HEADS)
    flip = lambda t: jnp.flip(t, axis=1)
    q, qc = jax.nn.silu(hs(q)), jax.nn.silu(hs(qc))
    i, ic = hs(i), hs(ic)
    lb_f = lb[0].reshape(HG_HEADS, HG_DK)
    lb_b = lb[1].reshape(HG_HEADS, HG_DK)
    k_f, lf_f = hgrn_forget(hs(f_fwd), lb_f)
    k_b, lf_b = hgrn_forget(hs(f_bwd), lb_b)
    kc_f, lfc_f = hgrn_forget(hs(fc_fwd), lb_f)
    kc_b, lfc_b = hgrn_forget(hs(fc_bwd), lb_b)
    b = qc.shape[0]
    if ctx_out:
        zeros = jnp.zeros((b, HG_HEADS, HG_DK, HG_DV), jnp.float32)
        oc_f, s_cf = gla_chunk_scan(qc, kc_f, ic, lfc_f, zeros)
        oc_b, s_cb = gla_chunk_scan(flip(qc), flip(kc_b), flip(ic), flip(lfc_b), zeros)
        yc = merge_heads(rms_norm_2(oc_f + flip(oc_b), norm_g))
    else:
        s_cf = gla_final_state(kc_f, ic, lfc_f)
        s_cb = gla_final_state(flip(kc_b), flip(ic), flip(lfc_b))
        yc = None
    o_f, _ = gla_chunk_scan(q, k_f, i, lf_f, s_cf)
    o_b, _ = gla_chunk_scan(flip(q), flip(k_b), flip(i), flip(lf_b), s_cb)
    y = merge_heads(rms_norm_2(o_f + flip(o_b), norm_g))
    return y, yc

def global_gqa(q, k, v, sink=None):
    b, s, h, d = q.shape
    kv = k.shape[2]
    g = h // kv
    scale = d ** -0.5
    qg = q.reshape(b, s, kv, g, d)

    def block(qb):
        logits = jnp.einsum('bqkgd,btkd->bkgqt', qb, k).astype(jnp.float32) * scale
        if sink is None:
            p = jax.nn.softmax(logits, axis=-1)
        else:
            col = jnp.broadcast_to(sink.astype(jnp.float32).reshape(kv, g)[None, :, :, None, None],
                                   logits.shape[:-1] + (1,))
            p = jax.nn.softmax(jnp.concatenate([logits, col], axis=-1), axis=-1)[..., :-1]
        return jnp.einsum('bkgqt,btkd->bqkgd', p.astype(v.dtype), v)

    return sweep_query_blocks(block, qg).reshape(b, s, h, d)

def diff_attention(q, k, v, lam, lam_init, subln_g):
    scale = q.shape[-1] ** -0.5

    def block(qb):
        logits = jnp.einsum('bqhmd,bthmd->bhmqt', qb, k).astype(jnp.float32) * scale
        p = jax.nn.softmax(logits, axis=-1)
        w = p[:, :, 0] - lam * p[:, :, 1]
        return jnp.einsum('bhqt,bthd->bqhd', w.astype(v.dtype), v)

    o = sweep_query_blocks(block, q)
    return rms_norm_2(o, subln_g) * (1.0 - lam_init)

def window_gqa_latent(q, k, v, k_ctx, v_ctx, sink):
    b, s, h, d = q.shape
    kv = k.shape[2]
    g = h // kv
    nb = s // Q_BLOCK
    scale = d ** -0.5

    def banded(t):
        tp = jnp.pad(t, ((0, 0), (Q_BLOCK, Q_BLOCK), (0, 0), (0, 0)))
        tb = tp.reshape(b, nb + 2, Q_BLOCK, kv, d)
        return jnp.concatenate([tb[:, :-2], tb[:, 1:-1], tb[:, 2:]], axis=2)

    kb, vb = banded(k), banded(v)
    qb = q.reshape(b, nb, Q_BLOCK, kv, g, d)
    blk = jnp.arange(nb)[:, None, None]
    qpos = blk * Q_BLOCK + jnp.arange(Q_BLOCK)[None, :, None]
    kpos = (blk - 1) * Q_BLOCK + jnp.arange(3 * Q_BLOCK)[None, None, :]
    allowed = (jnp.abs(kpos - qpos) <= WINDOW) & (kpos >= 0) & (kpos < s)
    lw = jnp.einsum('bnqkgd,bnskd->bnkgqs', qb, kb).astype(jnp.float32) * scale
    lw = jnp.where(allowed[None, :, None, None], lw, -jnp.inf)
    lc = jnp.einsum('bnqkgd,bskd->bnkgqs', qb, k_ctx).astype(jnp.float32) * scale
    ls = jnp.broadcast_to(sink.astype(jnp.float32).reshape(kv, g)[None, None, :, :, None, None],
                          lw.shape[:-1] + (1,))
    p = jax.nn.softmax(jnp.concatenate([lw, lc, ls], axis=-1), axis=-1).astype(v.dtype)
    n_w = 3 * Q_BLOCK
    n_c = k_ctx.shape[1]
    o = (jnp.einsum('bnkgqs,bnskd->bnqkgd', p[..., :n_w], vb)
         + jnp.einsum('bnkgqs,bskd->bnqkgd', p[..., n_w:n_w + n_c], v_ctx))
    return o.reshape(b, s, h, d)

def mixer_layer(x, cx, c, c_ctx, w_in, w_out, w_ada, b_ada, ln_g, ln_b, lb, hg_norm_g,
                ga_qn, ga_kn, df_lam, df_subln_g, wn_sink, rope64, rope32, layer_idx, ctx_out):
    alpha = (2.0 * DEPTH) ** 0.25
    shift, scale, gate = jnp.split(jax.nn.silu(c) @ w_ada + b_ada, 3, axis=-1)
    shift_c, scale_c, gate_c = jnp.split(jax.nn.silu(c_ctx) @ w_ada + b_ada, 3, axis=-1)
    h = x * (1.0 + scale[:, None]) + shift[:, None]
    hc = cx * (1.0 + scale_c) + shift_c
    (a_q, a_i, a_ff, a_fb, b_q, b_k, b_v, c_q, c_k, c_v, d_q, d_k, d_v, g_lat) = jnp.split(h @ w_in, SPLIT_AT, axis=-1)
    (a_qc, a_ic, a_ffc, a_fbc, b_qc, b_kc, b_vc, c_qc, c_kc, c_vc, d_qc, d_kc, d_vc, g_ctx) = jnp.split(hc @ w_in, SPLIT_AT, axis=-1)

    y_a, yc_a = hgrn2_mixer(a_q, a_i, a_ff, a_fb, a_qc, a_ic, a_ffc, a_fbc, lb, hg_norm_g, ctx_out)

    qB = apply_rope_2(rms_norm_2(split_heads(b_q, GA_HEADS), ga_qn), rope64)
    kB = apply_rope_2(rms_norm_2(split_heads(b_k, GA_KV), ga_kn), rope64)
    vB = split_heads(b_v, GA_KV)
    kBc = rms_norm_2(split_heads(b_kc, GA_KV), ga_kn)
    vBc = split_heads(b_vc, GA_KV)
    y_b = merge_heads(global_gqa(qB, jnp.concatenate([kB, kBc], 1), jnp.concatenate([vB, vBc], 1)))

    bsz, n = x.shape[0], x.shape[1]
    n_ctx = cx.shape[1]
    def diff_qk(t, length, rotate):
        t = t.reshape(bsz, length, DF_HEADS * 2, DF_QK)
        if rotate:
            t = apply_rope_2(t, rope32)
        return t.reshape(bsz, length, DF_HEADS, 2, DF_QK)
    lam_init = 0.8 - 0.6 * math.exp(-0.3 * layer_idx)
    lamf = df_lam.astype(jnp.float32)
    lam = jnp.exp(jnp.sum(lamf[0] * lamf[1])) - jnp.exp(jnp.sum(lamf[2] * lamf[3])) + lam_init
    qC, kC, vC = diff_qk(c_q, n, True), diff_qk(c_k, n, True), split_heads(c_v, DF_HEADS)
    kCc, vCc = diff_qk(c_kc, n_ctx, False), split_heads(c_vc, DF_HEADS)
    y_c = merge_heads(diff_attention(qC, jnp.concatenate([kC, kCc], 1), jnp.concatenate([vC, vCc], 1),
                                     lam, lam_init, df_subln_g))

    qD = apply_rope_2(split_heads(d_q, WN_HEADS), rope64)
    kD = apply_rope_2(split_heads(d_k, WN_KV), rope64)
    vD = split_heads(d_v, WN_KV)
    kDc, vDc = split_heads(d_kc, WN_KV), split_heads(d_vc, WN_KV)
    y_d = merge_heads(window_gqa_latent(qD, kD, vD, kDc, vDc, wn_sink))

    y = jnp.concatenate([y_a, y_b, y_c, y_d], axis=-1) * jax.nn.silu(g_lat)
    x_new = layer_norm(alpha * x + gate[:, None] * (y @ w_out), ln_g, ln_b)
    if not ctx_out:
        return x_new, None

    yc_b = merge_heads(global_gqa(rms_norm_2(split_heads(b_qc, GA_HEADS), ga_qn), kBc, vBc))
    yc_c = merge_heads(diff_attention(diff_qk(c_qc, n_ctx, False), kCc, vCc, lam, lam_init, df_subln_g))
    yc_d = merge_heads(global_gqa(split_heads(d_qc, WN_HEADS), kDc, vDc, wn_sink))
    yc = jnp.concatenate([yc_a, yc_b, yc_c, yc_d], axis=-1) * jax.nn.silu(g_ctx)
    cx_new = layer_norm(alpha * cx + gate_c * (yc @ w_out), ln_g, ln_b)
    return x_new, cx_new

def second_inputs(seed: int = 0) -> dict:
    key = jax.random.key(seed)
    ks = jax.random.split(key, 17)
    f32 = jnp.float32
    nrm = lambda k, shape, s: jax.random.normal(k, shape, f32) * s
    beta = (8.0 * DEPTH) ** -0.25
    return {
        "x": nrm(ks[0], (BATCH, SEQ, D_MODEL), 1.0),
        "c": nrm(ks[1], (BATCH, D_MODEL), 1.0),
        "ctx": nrm(ks[2], (BATCH, CTX_LEN, D_MODEL), 1.0),
        "c_ctx": nrm(ks[3], (D_MODEL,), 1.0),
        "w_in": nrm(ks[4], (DEPTH, D_MODEL, IN_WIDTH), D_MODEL ** -0.5),
        "w_out": nrm(ks[5], (DEPTH, D_MIX, D_MODEL), (D_MIX ** -0.5) * beta),
        "w_ada": nrm(ks[6], (DEPTH, D_MODEL, 3 * D_MODEL), 0.5 * D_MODEL ** -0.5),
        "b_ada": nrm(ks[7], (DEPTH, 3 * D_MODEL), 0.02),
        "ln_g": 1.0 + nrm(ks[8], (DEPTH, D_MODEL), 0.02),
        "ln_b": nrm(ks[9], (DEPTH, D_MODEL), 0.02),
        "hg_lb_logits": nrm(ks[10], (DEPTH, 2, HG_HEADS * HG_DK), 0.1),
        "hg_norm_g": 1.0 + nrm(ks[11], (DEPTH, HG_DV), 0.02),
        "ga_q_norm_g": 1.0 + nrm(ks[12], (DEPTH, HEAD_DIM), 0.02),
        "ga_k_norm_g": 1.0 + nrm(ks[13], (DEPTH, HEAD_DIM), 0.02),
        "df_lambda": nrm(ks[14], (DEPTH, 4, DF_QK), 0.1),
        "df_subln_g": 1.0 + nrm(ks[15], (DEPTH, DF_V), 0.02),
        "wn_sink": nrm(ks[16], (DEPTH, WN_HEADS), 0.5),
    }

def second_block(x, c, ctx, c_ctx, w_in, w_out, w_ada, b_ada, ln_g, ln_b, hg_lb_logits, hg_norm_g,
              ga_q_norm_g, ga_k_norm_g, df_lambda, df_subln_g, wn_sink):
    n = x.shape[1]
    rope64 = axial_rope(n, HEAD_DIM)
    rope32 = axial_rope(n, DF_QK)
    lb_sm = jax.nn.softmax(hg_lb_logits.astype(jnp.float32), axis=0)
    lower_bounds = jnp.cumsum(lb_sm, axis=0) - lb_sm[0]
    cx = ctx
    for l in range(DEPTH):
        x, cx = mixer_layer(x, cx, c, c_ctx, w_in[l], w_out[l], w_ada[l], b_ada[l], ln_g[l], ln_b[l],
                            lower_bounds[l], hg_norm_g[l], ga_q_norm_g[l], ga_k_norm_g[l], df_lambda[l],
                            df_subln_g[l], wn_sink[l], rope64, rope32, l, l < DEPTH - 1)
    return x


def setup_inputs(seed=0):
    out = dict(first_inputs(seed))
    for name, value in second_inputs(seed + 1).items():
        if name != "x":
            out[name + "_2"] = value
    return out


def reference(
    x, positions, norm_gain, ffn_w_gate, ffn_w_up, ffn_w_down, pool_w_in, pool_w_group,
    pool_scale, pool_w_out, kv_norm_gain, w_k, w_v, attn_w_q, attn_w_o, c_2, ctx_2, c_ctx_2,
    w_in_2, w_out_2, w_ada_2, b_ada_2, ln_g_2, ln_b_2, hg_lb_logits_2, hg_norm_g_2,
    ga_q_norm_g_2, ga_k_norm_g_2, df_lambda_2, df_subln_g_2, wn_sink_2,
):
    x = first_block(
        x, positions, norm_gain, ffn_w_gate, ffn_w_up, ffn_w_down, pool_w_in, pool_w_group,
        pool_scale, pool_w_out, kv_norm_gain, w_k, w_v, attn_w_q, attn_w_o,
    )
    return second_block(
        x, c_2, ctx_2, c_ctx_2, w_in_2, w_out_2, w_ada_2, b_ada_2, ln_g_2, ln_b_2,
        hg_lb_logits_2, hg_norm_g_2, ga_q_norm_g_2, ga_k_norm_g_2, df_lambda_2, df_subln_g_2,
        wn_sink_2,
    )


_drawn_inputs = setup_inputs


def setup_inputs(seed=0):
    import zlib

    import numpy as np

    out = dict(_drawn_inputs(seed))
    spreads = {}
    factors = {'ctx_2': 8.0,
     'c_ctx_2': 4.564,
     'b_ada_2': 7.286,
     'hg_lb_logits_2': 8.0,
     'hg_norm_g_2': 8.0,
     'ga_q_norm_g_2': 8.0,
     'ga_k_norm_g_2': 8.0,
     'df_lambda_2': 8.0,
     'df_subln_g_2': 8.0,
     'wn_sink_2': 8.0}
    for name, (base, spread) in spreads.items():
        noise = np.random.default_rng([zlib.crc32(name.encode()), seed]).standard_normal(out[name].shape)
        drawn = base * np.exp(spread * noise) if base else spread * noise
        out[name] = __import__('jax').numpy.asarray(drawn.astype(out[name].dtype))
    for name, factor in factors.items():
        out[name] = (out[name] * factor).astype(out[name].dtype)
    return out
```

```python
import math
from contextlib import ExitStack

import numpy as np

import concourse.bass as bass
from concourse import mybir
from concourse.alu_op_type import AluOpType as ALU

F32 = mybir.dt.float32
F32R = mybir.dt.float32r
BF16 = mybir.dt.bfloat16
I32 = mybir.dt.int32
ACT = mybir.ActivationFunctionType
AX = mybir.AxisListType

P = 128
D = 1024
KC = D // P
SEQ, CTX = 512, 256
TOK = SEQ + CTX
HALF = TOK // 2
D_FF = 2816
FC = D_FF // P
FF_PARTS = (8, 8, 6)
DEPTH = 2
EPS, LN_EPS = 1e-6, 1e-5
NEG = -1e30
HEAD = 64
A_WIN = (128, 128, 128)
A_DIL = (1, 4, 16)
A_HEADS = 8
GRID_W = 64
POOL_WINDOWS = (2, 4, 8, 16)
PAD = 16
LEVELS = 7
ALPHA = (2.0 * DEPTH) ** 0.25
NQ = TOK // P
LQ = SEQ // P
TILE = KC * P
RAW, SPLIT = 4, 2

PAR_WIDTHS = {
    "norm": DEPTH * 6 * KC, "kv": KC, "pscale": KC, "bada": DEPTH * 24, "lng": DEPTH * KC, "lnb": DEPTH * KC,
    "cc": 2 * KC, "lb": DEPTH * 4, "hgn": DEPTH, "gaq": DEPTH, "gak": DEPTH, "dfg": DEPTH,
    "sink": DEPTH * 4, "dfl": DEPTH * 4 * 32,
}
PAR_AT, _at = {}, 0
for _n, _w in PAR_WIDTHS.items():
    PAR_AT[_n] = _at
    _at += _w
NPAR = _at

CON_WIDTHS = {"ident": P, "ones": P, "blk": P, "rot32": P, "rot16": P, "rot8": P, "invf": 1, "cnt": 4 * PAD,
              "cos16": SEQ, "sin16": SEQ, "cos8": SEQ, "sin8": SEQ}
CON_AT, _at = {}, 0
for _n, _w in CON_WIDTHS.items():
    CON_AT[_n] = _at
    _at += _w
NCON = CON_AT["cos16"]
NTAB = _at - NCON
MASKS = ("ident", "g0diag", "g0prev", "g1diag", "g1off", "g2diag", "g2off", "wprev", "wnext", "blk32")
NMASK = len(MASKS) * P
NLOW = LEVELS - 1
BLK = 32
NLEV = 2 * NLOW * BLK


def constants():
    c = {}
    c["ident"] = np.eye(P)
    c["ones"] = np.ones((P, P))
    p = np.arange(P)
    c["blk"] = (p[:, None] // HEAD == p[None, :] // HEAD) * 1.0
    for h in (32, 16, 8):
        m = np.zeros((P, P))
        for d in range(P):
            first = (d // h) % 2 == 0
            m[d + h if first else d - h, d] = -1.0 if first else 1.0
        c[f"rot{h}"] = m
    inv = 10000.0 ** (-np.arange(0, HEAD, 2) / HEAD)
    c["invf"] = inv[p % 32][:, None]
    c["cnt"] = np.stack([np.broadcast_to(1.0 / np.minimum(np.arange(PAD) + 1, w), (P, PAD)) for w in POOL_WINDOWS], 1).reshape(P, -1)
    t = np.arange(SEQ)
    for h in (16, 8):
        axis = 2 * h
        inv = (10000.0 ** (-np.arange(0, axis, 2) / axis)).astype(np.float32)
        d = p % (4 * h)
        pos = np.where((d < axis)[:, None], (t // GRID_W)[None, :], (t % GRID_W)[None, :]).astype(np.float32)
        ang = (pos * inv[d % h][:, None]).astype(np.float32).astype(np.float64)
        c[f"cos{h}"], c[f"sin{h}"] = np.cos(ang), np.sin(ang)
    con = np.concatenate([c[n] for n in CON_WIDTHS], 1).astype(np.float32)
    q, k = p[:, None], p[None, :]
    m = {"ident": np.eye(P)}
    bias = lambda ok: np.where(ok, 0.0, NEG)
    m["g0diag"] = bias(k <= q)
    m["g0prev"] = bias(k >= q)
    for g, d in ((1, 4), (2, 16)):
        m[f"g{g}diag"] = bias((k <= q) & ((q - k) % d == 0))
        m[f"g{g}off"] = bias((q - k) % d == 0)
    m["wprev"] = bias(k >= q)
    m["wnext"] = bias(k <= q)
    m["blk32"] = (q // BLK == k // BLK) * 1.0
    masks = np.concatenate([m[n] for n in MASKS], 1)
    s, tt = p[:, None] % BLK, np.arange(BLK)[None, :]
    low = [s == tt] + [
        (s >> (l + 1) == tt >> (l + 1)) & ((s >> l) % 2 == 0) & ((tt >> l) % 2 == 1) for l in range(NLOW - 1)]
    back = [s == tt] + [
        (s >> (l + 1) == tt >> (l + 1)) & ((s >> l) % 2 == 1) & ((tt >> l) % 2 == 0) for l in range(NLOW - 1)]
    levels = np.stack([np.stack(low, 1), np.stack(back, 1)], 1).reshape(P, -1).astype(np.float32)
    return con, masks, levels


def tile_plan():
    plan = []

    def ffn(layer, i):
        f0 = 0
        for part in FF_PARTS:
            for j in range(part):
                plan.append(("cols", "ffn_w_gate", (layer, i), (f0 + j) * P))
                plan.append(("cols", "ffn_w_up", (layer, i), (f0 + j) * P))
            for m in range(KC):
                plan.append(("down", (layer, i), f0, part, m))
            f0 += part

    def pool():
        plan.extend(("cols", "pool_w_in", (0,), m * P) for m in range(KC))
        plan.extend(("group", g) for g in (0, 2))
        plan.extend(("cols", "pool_w_out", (0,), m * P) for m in range(KC))

    def attention():
        for hp in range(A_HEADS // 2):
            for g in range(3):
                plan.append(("cols", "attn_w_q", (0,), (g * 4 + hp) * P))
                plan.append(("cols", "w_k", (), (g * 4 + hp) * P))
                plan.append(("cols", "w_v", (), (g * 4 + hp) * P))
        plan.extend(("attn_o", m) for m in range(0, KC, 2))

    def mixers(layer):
        plan.extend(("cols", "w_ada_2", (layer,), m * P) for m in range(24))
        w = lambda c: plan.append(("cols", "w_in_2", (layer,), c * P))
        heads = lambda base, hp: plan.append(("heads", layer, base * P, hp))
        for hp in range(2):
            for c in (0, 2, 4, 6, 22):
                w(c + hp)
        for hp in range(2):
            if hp == 0:
                w(10), w(11)
            heads(8, hp), heads(24, hp)
        for hp in range(2):
            for c in (12, 14, 16, 26):
                w(c + hp)
        for hp in range(2):
            if hp == 0:
                w(20), w(21)
            heads(18, hp), heads(28, hp)
        plan.extend(("mix_o", layer, m) for m in range(KC))

    ffn(0, 0)
    pool()
    ffn(0, 1)
    ffn(1, 0)
    attention()
    ffn(1, 1)
    for layer in range(DEPTH):
        mixers(layer)
    return plan


NT = len(tile_plan())


def lay_out_tiles(a):
    out = np.zeros((NT, P, KC, P), np.float32)
    for n, t in enumerate(tile_plan()):
        if t[0] == "cols":
            w = a[t[1]][t[2]][:, t[3]:t[3] + P]
        elif t[0] == "down":
            w = a["ffn_w_down"][t[1]][t[2] * P:(t[2] + t[3]) * P, t[4] * P:(t[4] + 1) * P]
        elif t[0] == "heads":
            w = a["w_in_2"][t[1]][:, t[2]:t[2] + 2 * P].reshape(D, 4, HEAD)[:, [t[3], t[3] + 2]].reshape(D, P)
        elif t[0] == "mix_o":
            w = a["w_out_2"][t[1]][:, t[2] * P:(t[2] + 1) * P].reshape(4, 4, HEAD, P)
            w = np.stack([w[0], w[1][[0, 2, 1, 3]], w[2], w[3][[0, 2, 1, 3]]])
        elif t[0] == "group":
            w = a["pool_w_group"][0, t[1]:t[1] + 2].reshape(2, 2, P, 2, P).transpose(0, 3, 1, 2, 4)
        else:
            w = a["attn_w_o"][0][:, t[1] * P:(t[1] + 2) * P].reshape(4, P, 2, P).transpose(2, 0, 1, 3)
        w = w.reshape(-1, P, P)
        out[n, :, :len(w)] = w.transpose(1, 0, 2)
    return out.reshape(NT * P, TILE)


def lay_out_parameters(a):
    fm = lambda v: v.reshape(-1, P).T
    both = lambda v: np.concatenate([v, v], 1).T
    every = lambda v: np.broadcast_to(v.reshape(1, -1), (P, v.size))
    cc = np.stack([a["c_2"][0], a["c_ctx_2"]]).reshape(2, KC, P).transpose(2, 1, 0).reshape(P, -1)
    parts = {
        "norm": fm(a["norm_gain"]), "kv": fm(a["kv_norm_gain"]), "pscale": fm(a["pool_scale"]),
        "bada": fm(a["b_ada_2"]), "lng": fm(a["ln_g_2"]), "lnb": fm(a["ln_b_2"]), "cc": cc,
        "lb": fm(a["hg_lb_logits_2"]), "hgn": both(a["hg_norm_g_2"]), "gaq": both(a["ga_q_norm_g_2"]),
        "gak": both(a["ga_k_norm_g_2"]), "dfg": both(a["df_subln_g_2"]), "sink": every(a["wn_sink_2"]),
        "dfl": every(a["df_lambda_2"]),
    }
    return np.concatenate([parts[n] for n in PAR_WIDTHS], 1)


def dilated_units():
    units = []
    for i in range(LQ):
        for h in range(2):
            blocks = [(0, j, "g0diag" if j == i else "g0prev") for j in range(max(i - 1, 0), i + 1)]
            for g in (1, 2):
                blocks += [(g, j, f"g{g}diag" if j == i else f"g{g}off") for j in range(i + 1)]
            units.append((i, h, blocks))
    return units


def all_keys(i):
    return [(0, j, None) for j in (range(NQ) if i < LQ else range(LQ, NQ))]


def window_keys(i):
    near = [(0, j, {-1: "wprev", 0: None, 1: "wnext"}[j - i]) for j in range(i - 1, i + 2) if 0 <= j < LQ]
    return (near if i < LQ else []) + [(0, j, None) for j in range(LQ, NQ)]


class Tally:

    def __init__(self):
        self.n = {}

    def take(self, name, k=1):
        at = self.n.get(name, 0)
        self.n[name] = at + k
        return at

    def at(self, name):
        return self.n.get(name, 0)


WORK = 9216
CONST_LOADS = 4 + KC
MAGIC = 1.5 * 2.0 ** 23
C1, C2, C3 = 6.28125, 0.0019350051879882812, 3.0199159819567529e-07
PI_IN = 3.1415925


def build(nc, wts, par, con, tab, masks, levels, pos, x, ctx_in, out, scratch, stop=None):
    ctx = ExitStack()
    with ctx:
        def sb(name, shape, dt=F32):
            return ctx.enter_context(nc.sbuf_tensor(name, shape, dt))

        def sem(name):
            return ctx.enter_context(nc.semaphore(name))

        raw = sb("raw", [P, RAW, TILE])
        wh = sb("wh", [P, SPLIT, TILE], F32R)
        wl = sb("wl", [P, SPLIT, TILE], F32R)
        xh = sb("xh", [P, KC, TOK], F32R)
        xl = sb("xl", [P, KC, TOK], F32R)
        ah = sb("ah", [P, KC * TOK], F32R)
        al = sb("al", [P, KC * TOK], F32R)
        hc = sb("hc", [P, KC, TOK])
        tb = sb("tb", [P, NTAB])
        mk = sb("mk", [P, NMASK], BF16)
        lev = sb("lev", [P, 2, NLOW, BLK], BF16)
        pr = sb("pr", [P, NPAR])
        cn = sb("cn", [P, NCON])
        ada = sb("ada", [P, 24, 2])
        cch = sb("cch", [P, 2 * KC], F32R)
        ccl = sb("ccl", [P, 2 * KC], F32R)
        sm = sb("sm", [P, 256])
        work = sb("work", [P, WORK])
        ps = ctx.enter_context(nc.psum_tensor("ps", [P, 8, 512], F32))

        def col(name, i=0, n=1):
            return pr[:, PAR_AT[name] + i:PAR_AT[name] + i + n]

        def const(name, n=None):
            return cn[:, CON_AT[name]:CON_AT[name] + (n or CON_WIDTHS[name])]

        def mask(name):
            return mk[:, MASKS.index(name) * P:(MASKS.index(name) + 1) * P]

        ident, ones = const("ident"), const("ones")
        eps_c, ln_eps_c, one_c, pi2_c = sm[:, 0:1], sm[:, 1:2], sm[:, 2:3], sm[:, 3:4]
        mx, negm, den, rden = sm[:, 4:6], sm[:, 6:8], sm[:, 8:10], sm[:, 10:12]
        esink, lamc, lnlb, ln1lb = sm[:, 12:14], sm[:, 14:22], sm[:, 22:26], sm[:, 26:30]
        hs, sd = sm[:, 32:44], sm[:, 44:56]
        lt = sm[:, 64:96]

        def ahk(k, n=SEQ):
            return ah[:, k * n:(k + 1) * n]

        def alk(k, n=SEQ):
            return al[:, k * n:(k + 1) * n]

        def area(at, n):
            assert at + n <= WORK, (at, n)
            return work[:, at:at + n]

        fo = area(0, KC * SEQ).rearrange("p (k t) -> p k t", k=KC)
        sil = area(4096, 2 * SEQ).rearrange("p (s t) -> p s t", s=2)
        sq = area(5120, 2 * SEQ).rearrange("p (s t) -> p s t", s=2)
        tt = area(6144, 2 * SEQ).rearrange("p (s t) -> p s t", s=2)
        pads = tb[:, 0:3 * (PAD + SEQ)].rearrange("p (s t) -> p s t", s=3)
        qk1 = area(0, 6 * SEQ).rearrange("p (s t) -> p s t", s=6)
        v1 = area(3072, 3 * SEQ).rearrange("p (g t) -> p g t", g=3)
        cs1 = tb[:, 0:2 * SEQ].rearrange("p (s t) -> p s t", s=2)
        t1 = tb[:, 2 * SEQ:4 * SEQ].rearrange("p (s t) -> p s t", s=2)

        const_in, cond_in = sem("const_in"), sem("cond_in")
        raw_in = [sem(f"raw_in{s}") for s in range(RAW)]
        hi_done, lo_done = sem("hi_done"), sem("lo_done")
        tile_done = sem("tile_done")
        taken = sem("taken")
        sil_ready, a_ready, x_ready, h_ready = sem("sil_ready"), sem("a_ready"), sem("x_ready"), sem("h_ready")
        sq_ready, sq_used, rstd_ready = sem("sq_ready"), sem("sq_used"), sem("rstd_ready")
        act_own, dve_own = sem("act_own"), sem("dve_own")
        h0_out, h0_in = sem("h0_out"), sem("h0_in")
        d2p, d2a, a2d, a2p, p2d, p2a = (sem(n) for n in (
            "vector_to_tensor", "vector_to_scalar", "scalar_to_vector", "scalar_to_tensor",
            "tensor_to_vector", "tensor_to_scalar"))
        s_full, neg_ready, p_ready = sem("s_full"), sem("neg_ready"), sem("p_ready")
        pt_full, pt_act, pt_dve = sem("pt_full"), sem("pt_act"), sem("pt_dve")
        o_full, o_taken = sem("o_full"), sem("o_taken")
        stored = sem("stored")
        block = ctx.enter_context(nc.Block())

        HALVES = ((0, HALF), (HALF, HALF))
        PHASES = [("ffn", 0, 0), ("pool",), ("ffn", 0, 1), ("keep",), ("ffn", 1, 0), ("dilated",), ("ffn", 1, 1)]
        for layer in range(DEPTH):
            PHASES += [("ada", layer), ("scan", layer, 0), ("scan", layer, 1), ("attend", layer, "global", 0),
                       ("attend", layer, "global", 1), ("attend", layer, "diff", 0), ("attend", layer, "diff", 1),
                       ("attend", layer, "window", 0), ("attend", layer, "window", 1), ("mix", layer)]
        PHASES = PHASES[:stop]
        H_TOTAL = KC * (1 + sum(p[0] in ("ffn", "pool", "dilated", "mix") for p in PHASES))

        q2, sg2, o2 = area(0, TOK), area(TOK, TOK), area(2 * TOK, TOK)
        ta, tbuf = area(3 * TOK, 512), area(3 * TOK + 512, 512)
        sq2 = area(3 * TOK, TOK)
        k2, v2 = area(3 * TOK + 1024, TOK), area(4 * TOK + 1024, TOK)
        P2AT = 5 * TOK + 1024
        sq_q, sz, sk, sv, sg, so, sz2 = (area(i * TOK, TOK) for i in range(7))
        BT = 2 * P
        swl = area(7 * TOK, LEVELS * BT)
        swl_v = swl.rearrange("p (l t) -> p l t", l=LEVELS)
        se = area(7 * TOK, TOK)
        sw = area(8 * TOK, TOK)
        SX = 7 * TOK + LEVELS * BT
        qi, kd = area(SX, BT), area(SX + BT, BT)
        lowp = area(SX + 2 * BT, 2 * NLOW * BLK).rearrange("p (h l t) -> p h l t", h=2, l=NLOW)
        lows = area(SX + 2 * BT + 2 * NLOW * BLK, 2 * BLK).rearrange("p (h t) -> p h t", h=2)
        HX = SX + 2 * BT + 2 * NLOW * BLK + 2 * BLK
        near = area(HX, 2 * P).rearrange("p (h t) -> p h t", h=2)
        far = area(HX + 2 * P, 2 * P).rearrange("p (h t) -> p h t", h=2)
        state = area(HX + 4 * P, P)
        kdt = area(HX + 5 * P, P)

        def attention(kind):
            units = []
            if kind == "dilated":
                for i, h, blocks in dilated_units():
                    units.append(dict(i=i, part=HEAD * h, width=HEAD, blocks=blocks, h=h, add=False))
            else:
                for i in range(NQ):
                    for h in range(2):
                        keys = window_keys(i) if kind == "window" else all_keys(i)
                        for m in range(2 if kind == "diff" else 1):
                            w = HEAD // 2 if kind == "diff" else HEAD
                            units.append(dict(i=i, part=HEAD * h + w * m, width=w, blocks=keys, h=h, add=m == 1))
            return units

        def buffers(kind):
            if kind == "dilated":
                q = lambda u, g: qk1[u["part"]:u["part"] + u["width"], 2 * g, u["i"] * P:(u["i"] + 1) * P]
                k = lambda u, g, j, n: qk1[u["part"]:u["part"] + u["width"], 2 * g + 1, j * P:(j + n) * P]
                v = lambda u, g, j: v1[:, g, j * P + HEAD * u["h"]:j * P + HEAD * (u["h"] + 1)]
                p = [area(4608, 1280)]
                pt = [area(4608 + 1280 * (s + 1), 1280) for s in range(2)]
                o = t1.rearrange("p s t -> p (s t)")[:, 0:SEQ]
            else:
                q = lambda u, g: q2[u["part"]:u["part"] + u["width"], u["i"] * P:(u["i"] + 1) * P]
                k = lambda u, g, j, n: k2[u["part"]:u["part"] + u["width"], j * P:(j + n) * P]
                v = lambda u, g, j: v2[:, j * P + HEAD * u["h"]:j * P + HEAD * (u["h"] + 1)]
                p = [area(P2AT + TOK * s, TOK) for s in range(2)]
                pt = [area(P2AT + TOK * (s + 2), TOK) for s in range(2)]
                o = o2
            return q, k, v, p, pt, o

        def slot(i, unit):
            n = len(unit["blocks"]) * P
            at = 2 * 512 if i % 2 == 0 else 7 * 512 - max(n, 1024)
            return ps[:, :, :].rearrange("p b n -> p (b n)")[:, at:at + n]

        def over(unit):
            return len(unit["blocks"]) > 8

        def o_psum(i, kind):
            return ps[:, 7 if i % 2 or kind == "dilated" else 4, 0:HEAD]

        def groups(unit):
            n = len(unit["blocks"])
            return [range(a, min(a + 4, n)) for a in range(0, n, 4)]

        def pass_tiles(kind, hp):
            if kind == "diff":
                return "qkvg"
            return "kvqg" if hp == 0 else "qg"

        def level_views(v, l, way):
            n = 1 << l
            v = v.rearrange("p (a c) -> p a c", c=2 * n)
            at = n - 1 if way == 0 else n
            return v[:, :, 0:n], v[:, :, n:2 * n], v[:, :, at:at + 1].to_broadcast([P, v.shape[1], n])

        def far_products(way):
            out_ = []
            for l, s0, q0, n in ((6, 0, 64, 64), (5, 0, 32, 32), (5, 64, 96, 32)):
                if way:
                    s0, q0 = q0, s0
                out_.append((slice(s0, s0 + n), slice(q0, q0 + n), l))
            return out_

        def lnsq(k):
            return area(k % 2 * TOK, TOK)

        @block.sync
        def _(sp):
            for n in range(RAW):
                sp.dma_start(raw[:, n, :], wts[n * P:(n + 1) * P, :]).then_inc(raw_in[n], 16)
            with sp.Fori(0, NT // RAW - 1) as i:
                for j in range(RAW):
                    src = wts[bass.ds((i * RAW + (RAW + j)) * P, P), :]
                    sp.wait_ge(lo_done, i * RAW + (j + 1))
                    sp.dma_start(raw[:, j, :], src).then_inc(raw_in[j], 16)
            for n in range(NT // RAW * RAW, NT):
                sp.wait_ge(lo_done, n - RAW + 1)
                sp.dma_start(raw[:, n % RAW, :], wts[n * P:(n + 1) * P, :]).then_inc(raw_in[n % RAW], 16)
            for k in range(KC):
                sp.wait_ge(h_ready, H_TOTAL - KC + k + 1)
                sp.dma_start(out[k * P:(k + 1) * P, :], hc[:, k, 0:SEQ]).then_inc(stored, 16)
            sp.wait_ge(stored, 16 * KC)

        @block.gpsimd
        def _(pool):
            with pool.Fori(0, NT // RAW) as i:
                for j in range(RAW):
                    pool.wait_ge(hi_done, i * RAW + (j + 1))
                    pool.tensor_tensor(wl[:, j % SPLIT, :], raw[:, j, :], wh[:, j % SPLIT, :].bitcast(F32),
                                       ALU.subtract).then_inc(lo_done, 1)
            for n in range(NT // RAW * RAW, NT):
                pool.wait_ge(hi_done, n + 1)
                pool.tensor_tensor(wl[:, n % SPLIT, :], raw[:, n % RAW, :], wh[:, n % SPLIT, :].bitcast(F32),
                                   ALU.subtract).then_inc(lo_done, 1)

        @block.scalar
        def _(act):
            c = Tally()

            def own(ins):
                c.take("own")
                ins.then_inc(act_own, 1)
                act.wait_ge(act_own, c.at("own"))

            def give(ins, s, name):
                c.take(name)
                ins.then_inc(s, 1)

            def get(s, name, k=1):
                c.take(name, k)
                act.wait_ge(s, c.at(name))

            def hi(n):
                if n < NT:
                    act.wait_ge(raw_in[n % RAW], 16 * (n // RAW + 1))
                    act.activation(wh[:, n % SPLIT, :], raw[:, n % RAW, :], ACT.Copy).then_inc(hi_done, 1)

            def tile():
                n = c.take("tile")
                act.wait_ge(tile_done, n + 1)
                hi(n + 2)
                return n

            def tiles_loop(k):
                n0 = c.take("tile", k)
                loop_tiles(n0, k // 4, lambda i, j: None)

            def loop_tiles(n0, times, after):
                with act.Fori(0, times) as i:
                    for j in range(4):
                        act.wait_ge(tile_done, i * 4 + (n0 + j + 1))
                        m = n0 + j + 2
                        act.wait_ge(raw_in[m % RAW], i * 16 + 16 * (m // RAW + 1))
                        act.activation(wh[:, m % SPLIT, :], raw[:, m % RAW, :], ACT.Copy).then_inc(hi_done, 1)
                        after(i, j)

            def square(src):
                n = c.take("sq")
                if n >= 2:
                    act.wait_ge(sq_used, n - 1)
                act.activation(sq[:, n % 2, :], src, ACT.Square).then_inc(sq_ready, 1)

            def rstd(bank, scale=1.0 / D, bias=None):
                own(act.activation(bank, bank, ACT.Ln, bias=bias if bias is not None else eps_c, scale=scale))
                act.activation(bank, bank, ACT.Exp, scale=-0.5).then_inc(rstd_ready, 1)

            def norm_bank():
                return ps[:, 4 + c.take("norm") % 2, :]

            def norm(sem_, at, src):
                for k in range(KC):
                    act.wait_ge(sem_, at(k))
                    square(src(k))
                act.wait_ge(sq_used, c.at("sq"))
                rstd(norm_bank())

            def h_squares():
                base = c.at("h")
                norm(h_ready, lambda k: base + k + 1, lambda k: hc[:, k, 0:SEQ])

            def f_squares():
                n = c.at("tile")
                norm(taken, lambda k: n - KC + k + 1 + 4, lambda k: fo[:, k, :])

            def ffn(layer, i):
                h_squares()
                for part in FF_PARTS:
                    def silu(i, j):
                        if j % 2 == 0:
                            act.wait_ge(taken, i * 4 + (n0 + j + 1))
                            act.activation(sil[:, j // 2, :], ps[:, (n0 + j) % 4, :], ACT.Silu).then_inc(sil_ready, 1)
                    n0 = c.take("tile", 2 * part)
                    loop_tiles(n0, part // 2, silu)
                    if part != FF_PARTS[-1]:
                        tiles_loop(KC)
                for m in range(KC):
                    tile()
                    if m:
                        act.wait_ge(taken, c.at("tile") - 1 + 4)
                        square(fo[:, m - 1, :])
                act.wait_ge(taken, c.at("tile") + 4)
                square(fo[:, KC - 1, :])
                act.wait_ge(sq_used, c.at("sq"))
                rstd(norm_bank())
                c.take("h", KC)

            def pool():
                h_squares()
                tiles_loop(KC)
                tile(), tile()
                tiles_loop(KC)
                f_squares()
                c.take("h", KC)

            def keep():
                act.wait_ge(h_ready, c.at("h") + KC)
                act.dma_start(scratch, hc[:, :, 0:SEQ]).then_inc(h0_out, 16)

            def attend(kind, scale, sink=None):
                units = attention(kind)
                q, k, v, p, pt, o = buffers(kind)
                lag = 0 if kind == "dilated" else 1
                u0, g0 = c.at("unit"), c.at("group")
                ends = []
                for u in units:
                    ends.append(g0 + len(groups(u)) + (ends[-1] - g0 if ends else 0))

                def evacuate(i):
                    for b, blocks in enumerate(groups(units[i])):
                        c.take("group")
                        if b % 2 == 0:
                            act.wait_ge(pt_full, c.at("group"))
                            if i >= 2:
                                act.wait_ge(o_full, u0 + i - 1)
                            n = len(blocks) * P
                            act.activation(pt[i % 2][:, blocks[0] * P:blocks[0] * P + n],
                                           ps[:, (c.at("group") - 1) % 2, 0:n], ACT.Copy).then_inc(pt_act, 1)

                for i, u in enumerate(units):
                    n = len(u["blocks"]) * P
                    act.wait_ge(neg_ready, u0 + i + 1)
                    if i >= len(p):
                        act.wait_ge(pt_full, ends[i - len(p)])
                    if sink is not None:
                        own(act.activation(esink[:, i % 2:i % 2 + 1], sink(u), ACT.Exp, bias=negm[:, i % 2:i % 2 + 1]))
                    act.activation(p[i % len(p)][:, 0:n], slot(i, u), ACT.Exp, bias=negm[:, i % 2:i % 2 + 1],
                                   scale=scale, accum_out=den[:, i % 2:i % 2 + 1]).then_inc(p_ready, 1)
                    if i >= lag:
                        evacuate(i - lag)
                if lag:
                    evacuate(len(units) - 1)
                c.take("unit", len(units))

            def dilated():
                h_squares()
                act.dma_start(t1[:, 1, :].bitcast(I32), pos).then_inc(cond_in, 16)
                act.wait_ge(h0_out, 16)
                act.dma_start(fo, scratch).then_inc(h0_in, 16)
                for s in range(2):
                    get(d2a, "d2a")
                    give(act.activation(cs1[:, s, :], t1[:, 0, :], ACT.Sin), a2d, "a2d")
                norm(h0_in, lambda k: 16, lambda k: fo[:, k, :])
                for hp in range(A_HEADS // 2):
                    for j in range(9):
                        tile()
                    attend("dilated", HEAD ** -0.5)
                for m in range(0, KC, 2):
                    tile()
                n = c.at("tile")
                norm(taken, lambda k: n - 4 + k // 2 + 1 + 4, lambda k: fo[:, k, :])
                c.take("h", KC)

            def nsp(e):
                own(act.activation(e, e, ACT.Exp, scale=-1.0))
                give(act.activation(e, e, ACT.Ln, bias=one_c), a2d, "a2d")

            def ada_phase(layer):
                if layer == 0:
                    act.dma_start(hc[:, :, SEQ:TOK], ctx_in).then_inc(cond_in, 16)
                    act.dma_start(tb[:, :], tab).then_inc(cond_in, 16)
                    act.activation(col("cc", 0, 16), col("cc", 0, 16), ACT.Silu).then_inc(a2d, 1)
                    c.take("a2d")
                    get(d2a, "d2a")
                    nsp(lt[:, 8:12])
                    get(d2a, "d2a")
                    give(act.activation(lt[:, 16:16 + 2 * DEPTH], lt[:, 16:16 + 2 * DEPTH], ACT.Exp), a2d, "a2d")
                tiles_loop(24)

            def scan(layer, hp):
                for j in range(5):
                    n = tile()
                    if j in (0, 4):
                        act.wait_ge(taken, n + 1 + 4)
                        give(act.activation(sq_q if j == 0 else sg, sq_q if j == 0 else sg, ACT.Silu), a2d, "a2d")
                for way in range(2):
                    get(d2a, "d2a")
                    nsp(se)
                    get(d2a, "d2a")
                    give(act.activation(sk, sk, ACT.Exp, bias=0.0 if layer == 0 else ln1lb[:, way * 2 + hp:way * 2 + hp + 1]), a2d, "a2d")
                    if layer:
                        get(d2a, "d2a")
                        nsp(se)
                    for batch in ((2, 0, 1) if way == 0 else (2, 1, 0)):
                        b = slice(batch * BT, (batch + 1) * BT)
                        get(d2a, "d2a")
                        act.activation(qi, sz[:, b], ACT.Exp)
                        for j in range(2):
                            tl = slice(batch * BT + j * P, batch * BT + (j + 1) * P)
                            last = batch * BT + j * P + (P - 1 if way == 0 else 0)
                            ins = act.activation(kd[:, j * P:(j + 1) * P], sz[:, tl], ACT.Exp, scale=-1.0, bias=sz[:, last:last + 1])
                        give(ins, a2d, "a2d")
                        get(d2a, "d2a")
                        give(act.activation(swl, swl, ACT.Exp), a2d, "a2d")
                        for j in ((0, 1) if way == 0 else (1, 0)):
                            get(p2a, "p2a")
                            for rows, cols, l, *_ in far_products(way):
                                src = ps[rows, 6:8, cols.start:cols.stop]
                                ins = act.activation(far[rows, :, cols], src, ACT.Copy)
                            give(ins, a2p, "a2p")
                get(d2a, "d2a")
                own(act.activation(hs, hs, ACT.Ln, bias=eps_c, scale=1.0 / HEAD))
                give(act.activation(hs, hs, ACT.Exp, scale=-0.5), a2d, "a2d")

            def head_norm():
                get(d2a, "d2a")
                give(act.activation(sq2, cur[0], ACT.Square), a2p, "a2p")
                get(p2a, "p2a")
                b = ps[:, 6:8, 0:HALF]
                own(act.activation(b, b, ACT.Ln, bias=eps_c, scale=1.0 / HEAD))
                give(act.activation(b, b, ACT.Exp, scale=-0.5), a2d, "a2d")

            cur = [None]

            def attend_phase(layer, kind, hp):
                for what in pass_tiles(kind, hp):
                    n = tile()
                    if what == "g":
                        act.wait_ge(taken, n + 1 + 4)
                        give(act.activation(sg2, sg2, ACT.Silu), a2d, "a2d")
                    if what in "qk" and kind == "global":
                        cur[0] = q2 if what == "q" else k2
                        head_norm()
                if kind == "window":
                    attend(kind, HEAD ** -0.5, lambda u: col("sink", layer * 4 + 2 * u["h"] + hp))
                else:
                    attend(kind, (HEAD // 2 if kind == "diff" else HEAD) ** -0.5)
                if kind == "diff":
                    get(d2a, "d2a")
                    own(act.activation(hs, hs, ACT.Ln, bias=eps_c, scale=1.0 / HEAD))
                    give(act.activation(hs, hs, ACT.Exp, scale=-0.5), a2d, "a2d")

            def mix(layer):
                for m in range(KC):
                    tile()
                for k in range(KC):
                    get(d2a, "d2a")
                    if k >= 2:
                        get(p2a, "p2a")
                    give(act.activation(lnsq(k), hc[:, k, :], ACT.Square), a2p, "a2p")
                get(p2a, "p2a", 2)
                b = ps[:, 6:8, 0:HALF]
                own(act.activation(b, b, ACT.Ln, bias=ln_eps_c, scale=1.0 / D))
                give(act.activation(b, b, ACT.Exp, scale=-0.5), a2d, "a2d")
                c.take("h", KC)

            for dst, src in ((cn[:], con), (pr[:], par), (area(0, NMASK), masks), (area(NMASK, NLEV), levels)):
                act.dma_start(dst, src).then_inc(const_in, 16)
            for k in range(KC):
                act.dma_start(hc[:, k, 0:SEQ], x[k * P:(k + 1) * P, :]).then_inc(const_in, 16)
            act.wait_ge(const_in, CONST_LOADS * 16)
            hi(0), hi(1)
            run = dict(ffn=ffn, pool=pool, keep=keep, dilated=dilated, ada=ada_phase, scan=scan, attend=attend_phase, mix=mix)
            for name, *rest in PHASES:
                run[name](*rest)

        @block.tensor
        def _(pe):
            c = Tally()

            def give(ins, s, name):
                c.take(name)
                ins.then_inc(s, 1)

            def get(s, name, k=1):
                c.take(name, k)
                pe.wait_ge(s, c.at(name))

            def mm3(outs, s, k, hi, lo, cols, start, stop):
                for w, x_, first, last in ((wh, hi, start, False), (wh, lo, False, False), (wl, hi, False, stop)):
                    for out_, at in zip(outs, cols):
                        ins = pe.matmul(out_, w[:, s, k * P:(k + 1) * P], x_(k, at), start=first, stop=last)
                return ins

            def settle():
                if c.at("tile"):
                    pe.wait_ge(taken, c.at("tile") + 4)

            def tiles_loop(n0, times, kn, hi, lo):
                with pe.Fori(0, times) as i:
                    for j in range(4):
                        pe.wait_ge(lo_done, i * 4 + (n0 + j + 1))
                        pe.wait_ge(taken, i * 4 + (n0 + j + 1))
                        for k in range(kn):
                            ins = mm3([ps[:, (n0 + j) % 4, 0:SEQ]], (n0 + j) % SPLIT, k, hi, lo, [0], k == 0, k == kn - 1)
                        ins.then_inc(tile_done, 1)

            def chunks(k, kn, hi, lo):
                tiles_loop(c.take("tile", k), k // 4, kn, hi, lo)

            def tile():
                n = c.take("tile")
                pe.wait_ge(lo_done, n + 1)
                return n

            def pair():
                n = tile()
                pe.wait_ge(taken, n + 3)
                return n, [2 * (n % 2), 2 * (n % 2) + 1]

            x_hi = lambda k, at: xh[:, k, 0:SEQ]
            x_lo = lambda k, at: xl[:, k, 0:SEQ]
            a_hi = lambda k, at: ahk(k)
            a_lo = lambda k, at: alk(k)

            def add_squares(k):
                n = c.take("sq")
                if k == 0:
                    c.take("norm")
                pe.wait_ge(sq_ready, n + 1)
                pe.matmul(ps[:, 4 + (c.at("norm") - 1) % 2, :], ones, sq[:, n % 2, :],
                          start=k == 0, stop=k == KC - 1).then_inc(sq_used, 1)

            def norm():
                for k in range(KC):
                    add_squares(k)

            def wait_x():
                c.take("x", KC)
                pe.wait_ge(x_ready, c.at("x"))

            def wait_a(k):
                c.take("a", k)
                pe.wait_ge(a_ready, c.at("a"))

            def ffn(layer, i):
                norm()
                wait_x()
                settle()
                for part in FF_PARTS:
                    chunks(2 * part, KC, x_hi, x_lo)
                    wait_a(part)
                    if part != FF_PARTS[-1]:
                        chunks(KC, part, a_hi, a_lo)
                for m in range(KC):
                    n = tile()
                    pe.wait_ge(taken, n + 1)
                    for k in range(part):
                        ins = mm3([ps[:, n % 4, :]], n % SPLIT, k, a_hi, a_lo, [0], k == 0, k == part - 1)
                    ins.then_inc(tile_done, 1)
                    if m:
                        add_squares(m - 1)
                add_squares(KC - 1)

            def pool():
                norm()
                wait_x()
                chunks(KC, KC, x_hi, x_lo)
                wait_a(KC)
                for g2 in range(2):
                    n = tile()
                    settle_but_this(n)
                    for b in range(4):
                        g, m = 2 * g2 + b // 2, b % 2
                        for k in range(2):
                            blk = (b // 2) * 4 + m * 2 + k
                            for w, x_, first, last in ((wh, a_hi, k == 0, False), (wh, a_lo, False, False), (wl, a_hi, False, k == 1)):
                                ins = pe.matmul(ps[:, b, :], w[:, n % SPLIT, blk * P:(blk + 1) * P], x_(2 * g + k, 0), start=first, stop=last)
                    ins.then_inc(tile_done, 1)
                wait_x()
                settle()
                chunks(KC, KC, x_hi, x_lo)
                norm()

            def settle_but_this(n):
                pe.wait_ge(taken, n + 4)

            def attend(kind):
                units = attention(kind)
                q, k, v, p, pt, o = buffers(kind)
                lag = 0 if kind == "dilated" else 1
                u0 = c.at("unit")
                evacuated = c.n.setdefault("evacuated", [])

                def scores(i):
                    u = units[i]
                    if i >= 2:
                        pe.wait_ge(p_ready, u0 + i - 1)
                    if i >= 1 and over(u) and over(units[i - 1]):
                        pe.wait_ge(p_ready, u0 + i)
                    for b, (g, j, m) in enumerate(u["blocks"]):
                        out_ = slot(i, u)[:, b * P:(b + 1) * P]
                        ins = pe.matmul(out_, q(u, g), k(u, g, j, 1), start=True, stop=m is None)
                        if m is not None:
                            ins = pe.matmul(out_, mask("ident"), mask(m), start=False, stop=True)
                    ins.then_inc(s_full, 1)

                def transposes(i):
                    u = units[i]
                    pe.wait_ge(p_ready, u0 + i + 1)
                    for b, blocks in enumerate(groups(u)):
                        g = c.take("group")
                        name = "pt_act" if b % 2 == 0 else "pt_dve"
                        if len(evacuated) >= 2:
                            s, count = evacuated[-2]
                            pe.wait_ge(pt_act if s == "pt_act" else pt_dve, count)
                        c.take(name)
                        evacuated.append((name, c.at(name)))
                        for a, blk in enumerate(blocks):
                            ins = pe.transpose(ps[:, g % 2, a * P:(a + 1) * P], p[i % len(p)][:, blk * P:(blk + 1) * P], ident)
                        ins.then_inc(pt_full, 1)

                def values(i, last_group):
                    u = units[i]
                    for s, count in evacuated[last_group - len(groups(u)):last_group]:
                        pe.wait_ge(pt_act if s == "pt_act" else pt_dve, count)
                    back = 1 if kind == "dilated" else 2
                    if i >= back:
                        pe.wait_ge(o_taken, u0 + i - back + 1)
                    n = len(u["blocks"])
                    for b, (g, j, m) in enumerate(u["blocks"]):
                        ins = pe.matmul(o_psum(i, kind), pt[i % 2][:, b * P:(b + 1) * P], v(u, g, j), start=b == 0, stop=b == n - 1)
                    ins.then_inc(o_full, 1)

                scores(0)
                ends = []
                for i in range(len(units)):
                    if i + 1 < len(units):
                        scores(i + 1)
                    transposes(i)
                    ends.append(len(evacuated))
                    if i >= lag:
                        values(i - lag, ends[i - lag])
                if lag:
                    values(len(units) - 1, ends[-1])
                c.take("unit", len(units))

            def rotate(src, matrix):
                n = c.take("rot")
                give(pe.matmul(ps[:, 6 + n % 2, :], matrix, src, start=True, stop=True), p2d, "p2d")

            def turn_outputs(o, tiles, banks):
                for i in range(tiles):
                    at = (i % (tiles // len(banks))) * P
                    ins = pe.transpose(ps[:, banks[i // (tiles // len(banks))], at:at + P], o[:, i * P:(i + 1) * P], ident)
                give(ins, p2d, "p2d")

            def token_major(n, banks, hi, lo, tiles):
                per = tiles // len(banks)
                for t in range(tiles):
                    out_ = ps[:, banks[t // per], (t % per) * P:(t % per + 1) * P]
                    for k in range(KC):
                        for w, x_, first, last in ((wh, hi, k == 0, False), (wh, lo, False, False), (wl, hi, False, k == KC - 1)):
                            ins = pe.matmul(out_, x_(k, t * P, P), w[:, n % SPLIT, k * P:(k + 1) * P], start=first, stop=last)
                ins.then_inc(tile_done, 1)

            def dilated():
                norm()
                norm()
                wait_x()
                wait_a(KC)
                for hp in range(A_HEADS // 2):
                    settle()
                    for g in range(3):
                        for what in range(3):
                            n = tile()
                            pe.wait_ge(taken, n + 1)
                            if what == 2:
                                token_major(n, [n % 4], lambda k, at, w: ah[:, k * SEQ + at:k * SEQ + at + w],
                                            lambda k, at, w: al[:, k * SEQ + at:k * SEQ + at + w], LQ)
                            else:
                                hi, lo = (x_hi, x_lo) if what == 0 else (a_hi, a_lo)
                                for k in range(KC):
                                    ins = mm3([ps[:, n % 4, :]], n % SPLIT, k, hi, lo, [0], k == 0, k == KC - 1)
                                ins.then_inc(tile_done, 1)
                            if what:
                                pe.wait_ge(taken, n + 4)
                                rotate(qk1[:, 2 * g + what - 1, :], const("rot32"))
                    get(d2p, "d2p")
                    settle()
                    attend("dilated")
                    get(d2p, "d2p")
                    turn_outputs(buffers("dilated")[5], LQ, [4])
                wait_a(A_HEADS // 2)
                for m in range(0, KC, 2):
                    n, banks = pair()
                    for b in range(2):
                        for k in range(4):
                            blk = b * 4 + k
                            for w, x_, first, last in ((wh, ah, k == 0, False), (wh, al, False, False), (wl, ah, False, k == 3)):
                                ins = pe.matmul(ps[:, banks[b], :], w[:, n % SPLIT, blk * P:(blk + 1) * P],
                                                x_[:, (KC + k) * SEQ:(KC + k + 1) * SEQ], start=first, stop=last)
                    ins.then_inc(tile_done, 1)
                norm()

            def ada_phase(layer):
                settle()
                if layer == 0:
                    get(d2p, "d2p")
                n0 = c.take("tile", 24)
                with pe.Fori(0, 6) as i:
                    for j in range(4):
                        pe.wait_ge(lo_done, i * 4 + (n0 + j + 1))
                        pe.wait_ge(taken, i * 4 + (n0 + j + 1))
                        for k in range(KC):
                            ins = mm3([ps[:, (n0 + j) % 4, 0:2]], (n0 + j) % SPLIT, k,
                                      lambda k, at: cch[:, 2 * k:2 * k + 2], lambda k, at: ccl[:, 2 * k:2 * k + 2], [0], k == 0, k == KC - 1)
                        ins.then_inc(tile_done, 1)
                wait_x()
                settle()

            def wide(kn_hi, kn_lo):
                n, banks = pair()
                for k in range(KC):
                    ins = mm3([ps[:, b, 0:HALF] for b in banks], n % SPLIT, k, kn_hi, kn_lo, [a for a, _ in HALVES], k == 0, k == KC - 1)
                ins.then_inc(tile_done, 1)
                return n

            m_hi = lambda k, at: xh[:, k, at:at + HALF]
            m_lo = lambda k, at: xl[:, k, at:at + HALF]

            def values_tile():
                n, banks = pair()
                token_major(n, banks, lambda k, at, w: xh[:, k, at:at + w], lambda k, at, w: xl[:, k, at:at + w], NQ)
                return n

            def scan(layer, hp):
                for what in "qiffg":
                    values_tile() if what == "i" else wide(m_hi, m_lo)
                settle()
                for way in range(2):
                    for batch in ((2, 0, 1) if way == 0 else (2, 1, 0)):
                        get(d2p, "d2p")
                        for j in ((0, 1) if way == 0 else (1, 0)):
                            turn = c.take("scan tile") % 2
                            t0, gt = j * P, batch * BT + j * P
                            for h in range(2):
                                r = slice(HEAD * h, HEAD * (h + 1))
                                for l in range(NLOW):
                                    for b in range(P // BLK):
                                        if l == 0:
                                            kk, qq = sk[r, gt + b * BLK:gt + (b + 1) * BLK], sq_q[r, gt + b * BLK:gt + (b + 1) * BLK]
                                        else:
                                            kk = qq = swl_v[r, l - 1, t0 + b * BLK:t0 + (b + 1) * BLK]
                                        ins = pe.matmul(ps[b * BLK:(b + 1) * BLK, 4 + h, l * BLK:(l + 1) * BLK], kk, qq, start=True, stop=True)
                            give(ins, p2d, "p2d")
                            for h in range(2):
                                r = slice(HEAD * h, HEAD * (h + 1))
                                for rows, cols, l in far_products(way):
                                    ins = pe.matmul(ps[rows, 6 + h, cols], swl_v[r, l, t0 + rows.start:t0 + rows.stop],
                                                    swl_v[r, l, t0 + cols.start:t0 + cols.stop], start=True, stop=True)
                            give(ins, p2a, "p2a")
                            give(pe.transpose(ps[:, 2, 0:P], kd[:, t0:t0 + P], ident), p2d, "p2d")
                            get(d2p, "d2p", 2)
                            get(a2p, "a2p")
                            pe.matmul(ps[:, turn, 0:P], qi[:, t0:t0 + P], state, start=True, stop=False, skip_group_check=True)
                            for h in range(2):
                                vv = sv[:, gt + h * HEAD:gt + (h + 1) * HEAD]
                                oo = ps[:, turn, h * HEAD:(h + 1) * HEAD]
                                pe.matmul(oo, near[:, h, :], vv, start=False, stop=False, skip_group_check=True)
                                pe.matmul(oo, far[:, h, :], vv, start=False, stop=h == 1, skip_group_check=True)
                            give(pe.matmul(ps[:, 3, 0:P], kdt, sv[:, gt:gt + P], start=True, stop=True), p2d, "p2d")
                            c.take("d2p")
                get(d2p, "d2p")
                turn_outputs(so, NQ, [6, 7])

            def attend_phase(layer, kind, hp):
                for what in pass_tiles(kind, hp):
                    if what == "v":
                        values_tile()
                    else:
                        n = wide(m_hi, m_lo)
                    if what in "qk":
                        dst = q2 if what == "q" else k2
                        if kind == "global":
                            get(a2p, "a2p")
                            for b, (at, w) in enumerate(HALVES):
                                ins = pe.matmul(ps[:, 6 + b, 0:w], const("blk"), sq2[:, at:at + w], start=True, stop=True)
                            give(ins, p2a, "p2a")
                        get(d2p, "d2p")
                        give(pe.matmul(ps[:, 5, :], const("rot8" if kind == "diff" else "rot16"), dst[:, 0:SEQ], start=True, stop=True), p2d, "p2d")
                settle()
                get(d2p, "d2p")
                attend(kind)
                get(d2p, "d2p")
                turn_outputs(o2, NQ, [6, 7])

            def mix(layer):
                wait_a(KC)
                settle()
                for m in range(KC):
                    wide(lambda k, at: ah[:, k * TOK + at:k * TOK + at + HALF], lambda k, at: al[:, k * TOK + at:k * TOK + at + HALF])
                for k in range(KC):
                    get(d2p, "d2p")
                    for b, (at, w) in enumerate(HALVES):
                        ins = pe.matmul(ps[:, 4 + b, 0:w], ones, hc[:, k, at:at + w], start=k == 0, stop=k == KC - 1)
                give(ins, p2d, "p2d")
                for k in range(KC):
                    get(a2p, "a2p")
                    for b, (at, w) in enumerate(HALVES):
                        ins = pe.matmul(ps[:, 6 + b, 0:w], ones, lnsq(k)[:, at:at + w], start=k == 0, stop=k == KC - 1)
                    give(ins, p2a, "p2a")

            pe.wait_ge(const_in, CONST_LOADS * 16)
            run = dict(ffn=ffn, pool=pool, keep=lambda: None, dilated=dilated, ada=ada_phase, scan=scan, attend=attend_phase, mix=mix)
            for name, *rest in PHASES:
                run[name](*rest)

        @block.vector
        def _(dve):
            c = Tally()

            def own(ins):
                c.take("own")
                ins.then_inc(dve_own, 1)
                dve.wait_ge(dve_own, c.at("own"))

            def give(ins, s, name):
                c.take(name)
                ins.then_inc(s, 1)
                dve.wait_ge(s, c.at(name))

            def signal(s, name):
                c.take(name)
                dve.sem_inc(s, 1)

            def get(s, name, k=1):
                c.take(name, k)
                dve.wait_ge(s, c.at(name))

            def tile():
                n = c.take("tile")
                dve.wait_ge(tile_done, n + 1)
                return n

            def took(ins, n):
                ins.then_inc(taken, 1)
                dve.wait_ge(taken, n + 5)

            def split(src, hi, lo, s, name):
                own(dve.tensor_copy(hi, src))
                give(dve.tensor_tensor(lo, src, hi.bitcast(F32), ALU.subtract), s, name)

            def rstd():
                n = c.take("norm")
                dve.wait_ge(rstd_ready, c.take("rstd") + 1)
                return ps[:, 4 + n % 2, :]

            def to_x(src, gain, hi, lo, s, name):
                r = rstd()
                for k in range(KC):
                    t = tt[:, k % 2, :]
                    own(dve.scalar_tensor_tensor(t, src(k), gain(k), r, ALU.mult, ALU.mult))
                    split(t, hi(k), lo(k), s, name)

            def x_from_h(gain):
                to_x(lambda k: hc[:, k, 0:SEQ], gain, lambda k: xh[:, k, 0:SEQ], lambda k: xl[:, k, 0:SEQ], x_ready, "x")

            def add_f(gain):
                r = rstd()
                for k in range(KC):
                    t = tt[:, k % 2, :]
                    own(dve.scalar_tensor_tensor(t, fo[:, k, :], gain(k), r, ALU.mult, ALU.mult))
                    give(dve.tensor_tensor(hc[:, k, 0:SEQ], hc[:, k, 0:SEQ], t, ALU.add), h_ready, "h")

            def norm_gain(layer, i):
                return lambda k: col("norm", (layer * 6 + i) * KC + k)

            def down_loop(n0, first):
                with dve.Fori(0, KC // 4) as i:
                    for j in range(4):
                        dst = fo[:, bass.ds(i * 4 + j, 1), :].rearrange("p a t -> p (a t)")
                        src = ps[:, (n0 + j) % 4, :]
                        dve.wait_ge(tile_done, i * 4 + (n0 + j + 1))
                        if first:
                            dve.tensor_copy(dst, src).then_inc(taken, 1)
                        else:
                            dve.tensor_tensor(dst, dst, src, ALU.add).then_inc(taken, 1)
                dve.wait_ge(taken, n0 + KC + 4)

            def ffn_phase(layer, i):
                x_from_h(norm_gain(layer, 4 * i))
                for number, part in enumerate(FF_PARTS):
                    n0 = c.take("tile", 2 * part)
                    s0, o0, a0 = c.take("sil", part), c.take("own", part), c.take("a", part)
                    with dve.Fori(0, part // 2) as it:
                        for j in range(2):
                            hi = ah[:, bass.ds(it * (2 * SEQ) + j * SEQ, SEQ)]
                            lo = al[:, bass.ds(it * (2 * SEQ) + j * SEQ, SEQ)]
                            dve.wait_ge(sil_ready, it * 2 + (s0 + j + 1))
                            dve.wait_ge(tile_done, it * 4 + (n0 + 2 * j + 2))
                            dve.tensor_tensor(tt[:, j, :], sil[:, j, :], ps[:, (n0 + 2 * j + 1) % 4, :], ALU.mult).then_inc(taken, 2)
                            dve.wait_ge(taken, it * 4 + (n0 + 2 * j + 6))
                            dve.tensor_copy(hi, tt[:, j, :]).then_inc(dve_own, 1)
                            dve.wait_ge(dve_own, it * 2 + (o0 + j + 1))
                            dve.tensor_tensor(lo, tt[:, j, :], hi.bitcast(F32), ALU.subtract).then_inc(a_ready, 1)
                    dve.wait_ge(a_ready, a0 + part)
                    if number < len(FF_PARTS) - 1:
                        down_loop(c.take("tile", KC), number == 0)
                for m in range(KC):
                    n = tile()
                    took(dve.tensor_tensor(fo[:, m, :], fo[:, m, :], ps[:, n % 4, :], ALU.add), n)
                if (layer, i) == (1, 0):
                    dve.wait_ge(h0_out, 16)
                add_f(norm_gain(layer, 4 * i + 1))

            def pool():
                x_from_h(norm_gain(0, 2))
                own(dve.memset(pads[:, :, 0:PAD], 0.0))
                for m in range(KC):
                    n = tile()
                    w = POOL_WINDOWS[m // 2]
                    took(dve.tensor_copy(pads[:, 0, PAD:], ps[:, n % 4, :]), n)
                    step, src = 1, 0
                    while step < w:
                        dst = 1 if src != 1 else 2
                        own(dve.tensor_tensor(pads[:, dst, PAD:], pads[:, src, PAD:], pads[:, src, PAD - step:PAD + SEQ - step], ALU.add))
                        src, step = dst, 2 * step
                    t = tt[:, 0, :]
                    own(dve.scalar_tensor_tensor(t[:, PAD:], pads[:, src, 2 * PAD:], 1.0 / w, pads[:, 0, 2 * PAD:], ALU.mult, ALU.subtract))
                    cnt = const("cnt")[:, (m // 2) * PAD:(m // 2 + 1) * PAD]
                    own(dve.tensor_tensor(t[:, 0:PAD], pads[:, src, PAD:2 * PAD], cnt, ALU.mult))
                    own(dve.tensor_tensor(t[:, 0:PAD], t[:, 0:PAD], pads[:, 0, PAD:2 * PAD], ALU.subtract))
                    split(t, ahk(m), alk(m), a_ready, "a")
                for g2 in range(2):
                    n = tile()
                    for b in range(4):
                        m = g2 * 4 + b
                        t = tt[:, b % 2, :]
                        ins = dve.tensor_scalar(t, ps[:, b, :], col("pscale", m), None, ALU.mult)
                        took(ins, n) if b == 3 else own(ins)
                        split(t, xh[:, m, 0:SEQ], xl[:, m, 0:SEQ], x_ready, "x")
                down_loop(c.take("tile", KC), True)
                add_f(norm_gain(0, 3))

            def divide_round(t, u, v):
                own(dve.tensor_scalar(u, t, MAGIC, None, ALU.add))
                own(dve.tensor_scalar(v, u, MAGIC, None, ALU.subtract))

            def rope_tables():
                get_pos = t1[:, 1, :].bitcast(I32)
                dve.wait_ge(cond_in, 16)
                ang, u, v = tt[:, 0, :], tt[:, 1, :], sq[:, 0, :]
                own(dve.tensor_copy(sq[:, 1, :], get_pos))
                own(dve.tensor_scalar(ang, sq[:, 1, :], const("invf"), None, ALU.mult))
                for s in range(2):
                    own(dve.tensor_scalar(u, ang, 1.0 / (2 * math.pi), 0.25 if s == 0 else 0.0, ALU.mult, ALU.add))
                    divide_round(u, v, u)
                    own(dve.scalar_tensor_tensor(v, u, -C1, ang, ALU.mult, ALU.add))
                    own(dve.scalar_tensor_tensor(v, u, -C2, v, ALU.mult, ALU.add))
                    own(dve.scalar_tensor_tensor(v, u, -C3, v, ALU.mult, ALU.add))
                    if s == 0:
                        own(dve.tensor_scalar(v, v, math.pi / 2, None, ALU.add))
                    else:
                        get(a2d, "a2d")
                    give(dve.tensor_scalar(t1[:, 0, :], v, PI_IN, -PI_IN, ALU.min, ALU.max), d2a, "d2a")
                get(a2d, "a2d")

            def rope(dst, bank, cos, sin, a, b):
                own(dve.tensor_tensor(a, dst, cos, ALU.mult))
                own(dve.tensor_tensor(b, bank, sin, ALU.mult))
                own(dve.tensor_tensor(dst, a, b, ALU.add))

            def attend(kind, scale, sink=None, minus=None):
                units = attention(kind)
                q, k, v, p, pt, o = buffers(kind)
                lag = 0 if kind == "dilated" else 1
                u0 = c.at("unit")
                g_at = [c.at("group")]

                def maximum(i):
                    n = len(units[i]["blocks"]) * P
                    z = i % 2
                    dve.wait_ge(s_full, u0 + i + 1)
                    own(dve.tensor_reduce(mx[:, z:z + 1], slot(i, units[i]), AX.X, ALU.max))
                    if sink is None:
                        ins = dve.tensor_scalar(negm[:, z:z + 1], mx[:, z:z + 1], -scale, None, ALU.mult)
                    else:
                        own(dve.tensor_scalar(mx[:, z:z + 1], mx[:, z:z + 1], scale, sink(units[i]), ALU.mult, ALU.max))
                        ins = dve.tensor_scalar(negm[:, z:z + 1], mx[:, z:z + 1], -1.0, None, ALU.mult)
                    give(ins, neg_ready, "neg")

                def evacuate(i):
                    for b, blocks in enumerate(groups(units[i])):
                        g = c.take("group")
                        if b % 2:
                            dve.wait_ge(pt_full, g + 1)
                            if i >= 2:
                                dve.wait_ge(o_full, u0 + i - 1)
                            n = len(blocks) * P
                            give(dve.tensor_copy(pt[i % 2][:, blocks[0] * P:blocks[0] * P + n], ps[:, g % 2, 0:n]), pt_dve, "pt_dve")

                def output(i):
                    u, z = units[i], i % 2
                    dve.wait_ge(p_ready, u0 + i + 1)
                    if sink is not None:
                        own(dve.tensor_tensor(den[:, z:z + 1], den[:, z:z + 1], esink[:, z:z + 1], ALU.add))
                    own(dve.reciprocal(rden[:, z:z + 1], den[:, z:z + 1]))
                    dst = o[:, u["i"] * P + HEAD * u["h"]:u["i"] * P + HEAD * (u["h"] + 1)]
                    if u["add"]:
                        own(dve.tensor_scalar(rden[:, z:z + 1], rden[:, z:z + 1], minus, None, ALU.mult))
                    dve.wait_ge(o_full, u0 + i + 1)
                    if u["add"]:
                        ins = dve.scalar_tensor_tensor(dst, o_psum(i, kind), rden[:, z:z + 1], dst, ALU.mult, ALU.add)
                    else:
                        ins = dve.tensor_scalar(dst, o_psum(i, kind), rden[:, z:z + 1], None, ALU.mult)
                    give(ins, o_taken, "o_taken")

                if not lag:
                    maximum(0)
                for i in range(len(units)):
                    if lag:
                        maximum(i)
                    elif i + 1 < len(units):
                        maximum(i + 1)
                    if i >= lag:
                        evacuate(i - lag)
                        output(i - lag)
                if lag:
                    evacuate(len(units) - 1)
                    output(len(units) - 1)
                c.take("unit", len(units))

            def dilated():
                x_from_h(norm_gain(1, 2))
                rope_tables()
                to_x(lambda k: fo[:, k, :], lambda k: col("kv", k), ahk, alk, a_ready, "a")
                for hp in range(A_HEADS // 2):
                    for g in range(3):
                        for what in range(3):
                            n = tile()
                            dst = v1[:, g, :] if what == 2 else qk1[:, 2 * g + what, :]
                            took(dve.tensor_copy(dst, ps[:, n % 4, :]), n)
                            if what:
                                get(p2d, "p2d")
                                last = qk1[:, 2 * g + what - 1, :]
                                rope(last, ps[:, 6 + c.take("rot") % 2, :], cs1[:, 0, :], cs1[:, 1, :], t1[:, 0, :], t1[:, 1, :])
                    signal(d2p, "d2p")
                    attend("dilated", HEAD ** -0.5)
                    signal(d2p, "d2p")
                    get(p2d, "p2d")
                    split(ps[:, 4, :], ahk(KC + hp), alk(KC + hp), a_ready, "a")
                for m in range(0, KC, 2):
                    n = tile()
                    b = 2 * (n % 2)
                    took(dve.tensor_copy(fo[:, m:m + 2, :], ps[:, b:b + 2, :]), n)
                add_f(norm_gain(1, 3))

            def ada_phase(layer):
                if layer == 0:
                    get(a2d, "a2d")
                    split(col("cc", 0, 16), cch[:, :], ccl[:, :], d2p, "d2p")
                    own(dve.tensor_tensor(lt[:, 0:4], col("lb", 4, 4), col("lb", 0, 4), ALU.subtract))
                    give(dve.scalar_tensor_tensor(lt[:, 8:12], lt[:, 0:4], -1.0, lt[:, 0:4], ALU.mult, ALU.max), d2a, "d2a")
                    get(a2d, "a2d")
                    own(dve.tensor_scalar(lt[:, 4:8], lt[:, 0:4], -1.0, 0.0, ALU.mult, ALU.min))
                    own(dve.tensor_scalar(lt[:, 0:4], lt[:, 0:4], 0.0, None, ALU.min))
                    own(dve.tensor_tensor(lnlb, lt[:, 0:4], lt[:, 8:12], ALU.subtract))
                    own(dve.tensor_tensor(ln1lb, lt[:, 4:8], lt[:, 8:12], ALU.subtract))
                    for l in range(DEPTH):
                        for a in range(2):
                            one = col("dfl", (l * 4 + 2 * a) * 32, 32)
                            own(dve.tensor_tensor(one, one, col("dfl", (l * 4 + 2 * a + 1) * 32, 32), ALU.mult))
                            own(dve.tensor_reduce(lt[:, 16 + 2 * l + a:17 + 2 * l + a], one, AX.X, ALU.add))
                    signal(d2a, "d2a")
                    get(a2d, "a2d")
                    for l in range(DEPTH):
                        lam_init = 0.8 - 0.6 * math.exp(-0.3 * l)
                        own(dve.tensor_tensor(lamc[:, l:l + 1], lt[:, 17 + 2 * l:18 + 2 * l], lt[:, 16 + 2 * l:17 + 2 * l], ALU.subtract))
                        own(dve.tensor_scalar(lamc[:, l:l + 1], lamc[:, l:l + 1], -lam_init, None, ALU.add))
                        own(dve.tensor_scalar(col("dfg", l), col("dfg", l), 1.0 - lam_init, None, ALU.mult))
                    dve.wait_ge(cond_in, 48)
                n0 = c.take("tile", 24)
                with dve.Fori(0, 6) as i:
                    for j in range(4):
                        dst = ada[:, bass.ds(i * 4 + j, 1), :].rearrange("p a t -> p (a t)")
                        dve.wait_ge(tile_done, i * 4 + (n0 + j + 1))
                        dve.tensor_copy(dst, ps[:, (n0 + j) % 4, 0:2]).then_inc(taken, 1)
                dve.wait_ge(taken, n0 + 28)
                own(dve.tensor_tensor(ada[:, :, :], ada[:, :, :], col("bada", layer * 24, 24).unsqueeze(2).to_broadcast([P, 24, 2]), ALU.add))
                own(dve.tensor_scalar(ada[:, KC:2 * KC, :], ada[:, KC:2 * KC, :], 1.0, None, ALU.add))
                for k in range(KC):
                    t = area(k % 2 * TOK, TOK)
                    for s, (at, w) in enumerate(((0, SEQ), (SEQ, CTX))):
                        own(dve.tensor_scalar(t[:, at:at + w], hc[:, k, at:at + w], ada[:, KC + k, s:s + 1], ada[:, k, s:s + 1], ALU.mult, ALU.add))
                    split(t, xh[:, k, :], xl[:, k, :], x_ready, "x")

            def take_wide(dst):
                n = tile()
                b = 2 * (n % 2)
                took(dve.tensor_copy(dst.rearrange("p (b t) -> p b t", b=2), ps[:, b:b + 2, 0:HALF]), n)

            def finish(o_gate, gain, chunk):
                get(p2d, "p2d")
                t = area(3 * TOK, TOK)
                tv, bv = t.rearrange("p (b t) -> p b t", b=2), ps[:, 6:8, 0:HALF]
                gv = o_gate.rearrange("p (b t) -> p b t", b=2)
                if gain is None:
                    own(dve.tensor_tensor(tv, bv, gv, ALU.mult))
                else:
                    own(dve.scalar_tensor_tensor(tv, bv, gain, gv, ALU.mult, ALU.mult))
                split(t, ahk(chunk, TOK), alk(chunk, TOK), a_ready, "a")

            def head_rms(o, t):
                o3, t3 = (z.rearrange("p (h d) -> p h d", d=HEAD) for z in (o, t))
                own(dve.tensor_tensor(t, o, o, ALU.mult))
                give(dve.tensor_reduce(hs, t3, AX.X, ALU.add), d2a, "d2a")
                get(a2d, "a2d")
                give(dve.tensor_tensor(o3, o3, hs.unsqueeze(2).to_broadcast([P, 12, HEAD]), ALU.mult), d2p, "d2p")

            def log_forget(z, out_):
                give(dve.scalar_tensor_tensor(se, z, -1.0, z, ALU.mult, ALU.max), d2a, "d2a")
                get(a2d, "a2d")
                own(dve.scalar_tensor_tensor(out_, z, 0.0, se, ALU.min, ALU.subtract))

            def scan(layer, hp):
                for j, dst in enumerate((sq_q, sv, sz, sz2, sg)):
                    take_wide(dst)
                get(a2d, "a2d", 2)
                for way in range(2):
                    if way:
                        own(dve.tensor_copy(sz, sz2))
                    log_forget(sz, sw)
                    give(dve.tensor_tensor(sk, sw, sz, ALU.subtract), d2a, "d2a")
                    get(a2d, "a2d")
                    if layer:
                        own(dve.tensor_scalar(sz, sz, lnlb[:, way * 2 + hp:way * 2 + hp + 1], None, ALU.subtract))
                        log_forget(sz, sz)
                        own(dve.tensor_tensor(sz, sw, sz, ALU.subtract))
                    else:
                        own(dve.tensor_copy(sz, sw))
                    for t in range(NQ):
                        b = slice(t * P, (t + 1) * P)
                        own(dve.tensor_tensor_scan(sw[:, b], ones, sz[:, b], 0.0, ALU.mult, ALU.add))
                    if way == 0:
                        own(dve.tensor_copy(sz, sw))
                    else:
                        own(dve.tensor_tensor(sz, sz, sw, ALU.subtract))
                        for t in range(NQ):
                            b = slice(t * P, (t + 1) * P)
                            own(dve.tensor_scalar(sz[:, b], sz[:, b], sw[:, (t + 1) * P - 1:(t + 1) * P], None, ALU.add))
                    own(dve.memset(state, 0.0))
                    own(dve.memset(far, 0.0))
                    for batch in ((2, 0, 1) if way == 0 else (2, 1, 0)):
                        signal(d2a, "d2a")
                        zb = sz[:, batch * BT:(batch + 1) * BT]
                        for l in range(LEVELS):
                            first, second, border = level_views(zb, l, way)
                            w1, w2, _ = level_views(swl_v[:, l, :], l, way)
                            up, down = (first, second) if way == 0 else (second, first)
                            wu, wd = (w1, w2) if way == 0 else (w2, w1)
                            own(dve.tensor_tensor(wu, border, up, ALU.subtract))
                            own(dve.tensor_tensor(wd, down, border, ALU.subtract))
                        signal(d2a, "d2a")
                        get(a2d, "a2d")
                        for j in range(2):
                            last = j * P + (P - 1 if way == 0 else 0)
                            own(dve.tensor_copy(sd[:, j:j + 1], qi[:, last:last + 1]))
                        bt = slice(batch * BT, (batch + 1) * BT)
                        own(dve.tensor_tensor(qi, qi, sq_q[:, bt], ALU.mult))
                        own(dve.tensor_tensor(kd, kd, sk[:, bt], ALU.mult))
                        get(a2d, "a2d")
                        for l in range(LEVELS):
                            w1, w2, _ = level_views(swl_v[:, l, :], l, way)
                            wu, wd = (w1, w2) if way == 0 else (w2, w1)
                            k1_, k2_, _ = level_views(sk[:, bt], l, way)
                            q1_, q2_, _ = level_views(sq_q[:, bt], l, way)
                            own(dve.tensor_tensor(wu, wu, k1_ if way == 0 else k2_, ALU.mult))
                            own(dve.tensor_tensor(wd, wd, q2_ if way == 0 else q1_, ALU.mult))
                        signal(d2p, "d2p")
                        for j in ((0, 1) if way == 0 else (1, 0)):
                            turn = c.take("scan tile") % 2
                            gt = batch * BT + j * P
                            get(p2d, "p2d")
                            for h in range(2):
                                pv = ps[:, 4 + h, 0:NLOW * BLK].rearrange("p (l t) -> p l t", l=NLOW)
                                own(dve.tensor_tensor(lowp[:, h], pv, lev[:, way], ALU.mult))
                            own(dve.tensor_reduce(lows, lowp.rearrange("p h l t -> p h t l"), AX.X, ALU.add))
                            for h in range(2):
                                ins = dve.tensor_tensor(near[:, h, :].rearrange("p (b t) -> p b t", b=P // BLK),
                                                        lows[:, h, :].unsqueeze(1).to_broadcast([P, P // BLK, BLK]),
                                                        mask("blk32").rearrange("p (b t) -> p b t", b=P // BLK), ALU.mult)
                                give(ins, d2p, "d2p") if h else own(ins)
                            get(p2d, "p2d")
                            give(dve.tensor_copy(kdt, ps[:, 2, 0:P]), d2p, "d2p")
                            get(p2d, "p2d")
                            if way == 0:
                                own(dve.tensor_copy(so[:, gt:gt + P], ps[:, turn, 0:P]))
                            else:
                                own(dve.tensor_tensor(so[:, gt:gt + P], so[:, gt:gt + P], ps[:, turn, 0:P], ALU.add))
                            for h in range(2):
                                r = slice(HEAD * h, HEAD * (h + 1))
                                sh = state[r, h * HEAD:(h + 1) * HEAD]
                                ins = dve.scalar_tensor_tensor(sh, sh, sd[r, j:j + 1], ps[r, 3, h * HEAD:(h + 1) * HEAD], ALU.mult, ALU.add)
                                give(ins, d2p, "d2p") if h else own(ins)
                head_rms(so, sw)
                finish(sg, col("hgn", layer), hp)

            def attend_phase(layer, kind, hp):
                for what in pass_tiles(kind, hp):
                    dst = dict(q=q2, k=k2, v=v2, g=sg2)[what]
                    take_wide(dst)
                    if what in "qk":
                        if kind == "global":
                            signal(d2a, "d2a")
                            get(a2d, "a2d")
                            dv = dst.rearrange("p (b t) -> p b t", b=2)
                            own(dve.scalar_tensor_tensor(dv, dv, col("gaq" if what == "q" else "gak", layer), ps[:, 6:8, 0:HALF], ALU.mult, ALU.mult))
                        signal(d2p, "d2p")
                        get(p2d, "p2d")
                        z = 2 * SEQ if kind == "diff" else 0
                        rope(dst[:, 0:SEQ], ps[:, 5, :], tb[:, z:z + SEQ], tb[:, z + SEQ:z + 2 * SEQ], ta, tbuf)
                get(a2d, "a2d")
                signal(d2p, "d2p")
                if kind == "window":
                    attend(kind, HEAD ** -0.5, lambda u: col("sink", layer * 4 + 2 * u["h"] + hp))
                else:
                    attend(kind, (HEAD // 2 if kind == "diff" else HEAD) ** -0.5, minus=lamc[:, layer:layer + 1])
                if kind == "diff":
                    head_rms(o2, area(3 * TOK, TOK))
                else:
                    signal(d2p, "d2p")
                finish(sg2, col("dfg", layer) if kind == "diff" else None, 2 * ["scan", "global", "diff", "window"].index(kind) + hp)

            def mix(layer):
                for m in range(KC):
                    t = area((4 + m % 2) * TOK, TOK)
                    take_wide(t)
                    for s, (at, w) in enumerate(((0, SEQ), (SEQ, CTX))):
                        own(dve.tensor_scalar(t[:, at:at + w], t[:, at:at + w], ada[:, 2 * KC + m, s:s + 1], None, ALU.mult))
                    give(dve.scalar_tensor_tensor(hc[:, m, :], hc[:, m, :], ALPHA, t, ALU.mult, ALU.add), d2p, "d2p")
                get(p2d, "p2d")
                for k in range(KC):
                    hv = hc[:, k, :].rearrange("p (b t) -> p b t", b=2)
                    give(dve.scalar_tensor_tensor(hv, ps[:, 4:6, 0:HALF], -1.0 / D, hv, ALU.mult, ALU.add), d2a, "d2a")
                get(a2d, "a2d")
                for k in range(KC):
                    hv = hc[:, k, :].rearrange("p (b t) -> p b t", b=2)
                    own(dve.scalar_tensor_tensor(hv, hv, col("lng", layer * KC + k), ps[:, 6:8, 0:HALF], ALU.mult, ALU.mult))
                    give(dve.tensor_scalar(hc[:, k, :], hc[:, k, :], col("lnb", layer * KC + k), None, ALU.add), h_ready, "h")

            dve.wait_ge(const_in, CONST_LOADS * 16)
            own(dve.tensor_copy(mk[:, :], area(0, NMASK)))
            own(dve.tensor_copy(lev.rearrange("p a l t -> p (a l t)"), area(NMASK, NLEV)))
            own(dve.memset(eps_c, EPS))
            own(dve.memset(ln_eps_c, LN_EPS))
            own(dve.memset(one_c, 1.0))
            for layer in range(DEPTH):
                for i in (1, 5):
                    g = col("norm", (layer * 6 + i) * KC, KC)
                    own(dve.tensor_scalar(g, g, 0.5, None, ALU.mult))
            dve.sem_inc(taken, 4)
            dve.sem_inc(h_ready, KC)
            c.take("h", KC)
            run = dict(ffn=ffn_phase, pool=pool, keep=lambda: None, dilated=dilated, ada=ada_phase, scan=scan, attend=attend_phase, mix=mix)
            for name, *rest in PHASES:
                run[name](*rest)


_PROGRAM_INPUTS = ("wts", "par", "con", "tab", "masks", "levels", "pos", "x", "ctx")


def lay_out(inputs):
    a = {k: np.asarray(v) for k, v in inputs.items()}
    con, masks, levels = constants()
    return {
        "wts": lay_out_tiles(a),
        "par": np.ascontiguousarray(lay_out_parameters(a)),
        "con": np.ascontiguousarray(con[:, :NCON]),
        "tab": np.ascontiguousarray(con[:, NCON:]),
        "masks": masks.astype(np.float32),
        "levels": levels,
        "pos": np.ascontiguousarray(np.broadcast_to(a["positions"], (P, SEQ))),
        "x": np.ascontiguousarray(a["x"][0].T),
        "ctx": np.ascontiguousarray(a["ctx_2"][0].T.reshape(KC, P, CTX).transpose(1, 0, 2)),
    }


def program(nc, arrays, stop=None):
    args = []
    for name in _PROGRAM_INPUTS:
        v = arrays[name]
        args.append(nc.dram_tensor(name + "_dram", v.shape, mybir.dt.from_np(v.dtype), kind="ExternalInput").ap())
    out = nc.dram_tensor("out_dram", (D, SEQ), F32, kind="ExternalOutput").ap()
    scratch = nc.dram_tensor("kept_dram", (P, KC, SEQ), F32, kind="Internal").ap()
    build(nc, *args, out, scratch, stop=stop)


def kernel(**inputs):
    import concourse.bacc as bacc
    from concourse.bass_utils import run_bass_kernel_spmd

    nc = bacc.Bacc("TRN2", target_bir_lowering=False, num_devices=1)
    arrays = lay_out(inputs)
    program(nc, arrays)
    r = run_bass_kernel_spmd(nc, [{k + "_dram": v for k, v in arrays.items()}], core_ids=[0])
    return np.ascontiguousarray(r.results[0]["out_dram"].T)[None]
```

```python
import math
from contextlib import ExitStack, nullcontext

import numpy as np

import concourse.bass as bass
from concourse import mybir
from concourse.alu_op_type import AluOpType as ALU

F32 = mybir.dt.float32
F32R = mybir.dt.float32r
BF16 = mybir.dt.bfloat16
I32 = mybir.dt.int32
ACT = mybir.ActivationFunctionType
AX = mybir.AxisListType

P = 128
D = 1024
KC = D // P
SEQ, CTX = 512, 256
TOK = SEQ + CTX
HALF = TOK // 2
D_FF = 2816
FC = D_FF // P
FF_PARTS = (8, 8, 6)
DEPTH = 2
EPS, LN_EPS = 1e-6, 1e-5
NEG = -1e30
HEAD = 64
A_WIN = (128, 128, 128)
A_DIL = (1, 4, 16)
A_HEADS = 8
GRID_W = 64
POOL_WINDOWS = (2, 4, 8, 16)
PAD = 16
LEVELS = 7
ALPHA = (2.0 * DEPTH) ** 0.25
NQ = TOK // P
LQ = SEQ // P
TILE = KC * P
RAW, SPLIT = 4, 2
FOUR = 4 * P
GROUPS = DEPTH * 3 * D // FOUR
ADA_FFNS = ((0, 1), (1, 0), (1, 1))

PAR_WIDTHS = {
    "norm": DEPTH * 6 * KC, "kv": KC, "pscale": KC, "bada": DEPTH * 24, "lng": DEPTH * KC, "lnb": DEPTH * KC,
    "cc": 2 * KC, "lb": DEPTH * 4, "hgn": DEPTH, "gaq": DEPTH, "gak": DEPTH, "dfg": DEPTH,
    "sink": DEPTH * 4, "dfl": DEPTH * 4 * 32,
}
PAR_AT, _at = {}, 0
for _n, _w in PAR_WIDTHS.items():
    PAR_AT[_n] = _at
    _at += _w
NPAR = _at

CON_WIDTHS = {"ident": P, "ones": P, "blk": P, "rot32": P, "rot16": P, "rot8": P, "invf": 1, "cnt": 4 * PAD,
              "cos16": SEQ, "sin16": SEQ, "cos8": SEQ, "sin8": SEQ}
CON_AT, _at = {}, 0
for _n, _w in CON_WIDTHS.items():
    CON_AT[_n] = _at
    _at += _w
NCON = CON_AT["cos16"]
NTAB = _at - NCON
MASKS = ("ident", "g0diag", "g0prev", "g1diag", "g1off", "g2diag", "g2off", "wprev", "wnext", "blk32")
NMASK = len(MASKS) * P
NLOW = LEVELS - 1
BLK = 32
NLEV = 2 * NLOW * BLK


def constants():
    c = {}
    c["ident"] = np.eye(P)
    c["ones"] = np.ones((P, P))
    p = np.arange(P)
    c["blk"] = (p[:, None] // HEAD == p[None, :] // HEAD) * 1.0
    for h in (32, 16, 8):
        m = np.zeros((P, P))
        for d in range(P):
            first = (d // h) % 2 == 0
            m[d + h if first else d - h, d] = -1.0 if first else 1.0
        c[f"rot{h}"] = m
    inv = 10000.0 ** (-np.arange(0, HEAD, 2) / HEAD)
    c["invf"] = inv[p % 32][:, None]
    c["cnt"] = np.stack([np.broadcast_to(1.0 / np.minimum(np.arange(PAD) + 1, w), (P, PAD)) for w in POOL_WINDOWS], 1).reshape(P, -1)
    t = np.arange(SEQ)
    for h in (16, 8):
        axis = 2 * h
        inv = (10000.0 ** (-np.arange(0, axis, 2) / axis)).astype(np.float32)
        d = p % (4 * h)
        pos = np.where((d < axis)[:, None], (t // GRID_W)[None, :], (t % GRID_W)[None, :]).astype(np.float32)
        ang = (pos * inv[d % h][:, None]).astype(np.float32).astype(np.float64)
        c[f"cos{h}"], c[f"sin{h}"] = np.cos(ang), np.sin(ang)
    con = np.concatenate([c[n] for n in CON_WIDTHS], 1).astype(np.float32)
    q, k = p[:, None], p[None, :]
    m = {"ident": np.eye(P)}
    bias = lambda ok: np.where(ok, 0.0, NEG)
    m["g0diag"] = bias(k <= q)
    m["g0prev"] = bias(k >= q)
    for g, d in ((1, 4), (2, 16)):
        m[f"g{g}diag"] = bias((k <= q) & ((q - k) % d == 0))
        m[f"g{g}off"] = bias((q - k) % d == 0)
    m["wprev"] = bias(k >= q)
    m["wnext"] = bias(k <= q)
    m["blk32"] = (q // BLK == k // BLK) * 1.0
    masks = np.concatenate([m[n] for n in MASKS], 1)
    s, tt = p[:, None] % BLK, np.arange(BLK)[None, :]
    low = [s == tt] + [
        (s >> (l + 1) == tt >> (l + 1)) & ((s >> l) % 2 == 0) & ((tt >> l) % 2 == 1) for l in range(NLOW - 1)]
    back = [s == tt] + [
        (s >> (l + 1) == tt >> (l + 1)) & ((s >> l) % 2 == 1) & ((tt >> l) % 2 == 0) for l in range(NLOW - 1)]
    levels = np.stack([np.stack(low, 1), np.stack(back, 1)], 1).reshape(P, -1).astype(np.float32)
    return con, masks, levels


def tile_plan():
    plan = []

    def ffn(layer, i):
        f0 = 0
        for part in FF_PARTS:
            for j in range(part):
                plan.append(("cols", "ffn_w_gate", (layer, i), (f0 + j) * P))
                plan.append(("cols", "ffn_w_up", (layer, i), (f0 + j) * P))
            for m in range(KC):
                plan.append(("down", (layer, i), f0, part, m))
                if (layer, i) in ADA_FFNS and part != FF_PARTS[-1]:
                    n = sum(t[0] == "ada" for t in plan)
                    plan.append(("ada", n // 4, n % 4))
            f0 += part

    def pool():
        plan.extend(("cols", "pool_w_in", (0,), m * P) for m in range(KC))
        plan.extend(("group", g) for g in (0, 2))
        plan.extend(("cols", "pool_w_out", (0,), m * P) for m in range(KC))

    def attention():
        for hp in range(A_HEADS // 2):
            for g in range(3):
                plan.append(("cols", "attn_w_q", (0,), (g * 4 + hp) * P))
                plan.append(("cols", "w_k", (), (g * 4 + hp) * P))
                plan.append(("cols", "w_v", (), (g * 4 + hp) * P))
        plan.extend(("attn_o", m) for m in range(0, KC, 2))

    def mixers(layer):
        w = lambda c: plan.append(("cols", "w_in_2", (layer,), c * P))
        heads = lambda base, hp: plan.append(("heads", layer, base * P, hp))
        for hp in range(2):
            for c in (0, 22, 4, 2, 6):
                w(c + hp)
        for hp in range(2):
            if hp == 0:
                w(10), w(11)
            heads(8, hp), heads(24, hp)
        for hp in range(2):
            for c in (12, 14, 16, 26):
                w(c + hp)
        w(20), w(21)
        heads(18, 0), heads(28, 0), heads(28, 1), heads(18, 1)
        plan.extend(("mix_o", layer, m) for m in range(KC))

    ffn(0, 0)
    pool()
    ffn(0, 1)
    ffn(1, 0)
    attention()
    ffn(1, 1)
    for layer in range(DEPTH):
        mixers(layer)
    return plan


IS_ADA = [t[0] == "ada" for t in tile_plan()]
NT = len(IS_ADA)
LOADED = [n for n, ada in enumerate(IS_ADA) if not ada]
NS = len(LOADED)


def even_runs(first, blocks):
    at = lambda b: [LOADED[first + 4 * b + j] for j in range(4)]
    b = 0
    while b < blocks:
        e, step = b + 1, None
        while e < blocks:
            d = {y - x for x, y in zip(at(e - 1), at(e))}
            if d not in ({4}, {8}) or (step is not None and d != {step}):
                break
            step = min(d)
            e += 1
        yield b, e - b, step or 4
        b = e


def turns(engine, times):
    return engine.Fori(0, times) if times > 1 else nullcontext(0)


def lay_out_tiles(a):
    out = np.zeros((NT, P, KC, P), np.float32)
    for n, t in enumerate(tile_plan()):
        if t[0] == "cols":
            w = a[t[1]][t[2]][:, t[3]:t[3] + P]
        elif t[0] == "down":
            w = a["ffn_w_down"][t[1]][t[2] * P:(t[2] + t[3]) * P, t[4] * P:(t[4] + 1) * P]
        elif t[0] == "ada":
            layer, at = divmod(t[1] * FOUR, 3 * D)
            w = a["w_ada_2"][layer][t[2] * 2 * P:(t[2] + 1) * 2 * P, at:at + FOUR].reshape(2, P, 4, P).transpose(0, 2, 1, 3)
        elif t[0] == "heads":
            w = a["w_in_2"][t[1]][:, t[2]:t[2] + 2 * P].reshape(D, 4, HEAD)[:, [t[3], t[3] + 2]].reshape(D, P)
        elif t[0] == "mix_o":
            w = a["w_out_2"][t[1]][:, t[2] * P:(t[2] + 1) * P].reshape(4, 4, HEAD, P)
            w = np.stack([w[0], w[1][[0, 2, 1, 3]], w[2], w[3][[0, 2, 1, 3]]])
        elif t[0] == "group":
            w = a["pool_w_group"][0, t[1]:t[1] + 2].reshape(2, 2, P, 2, P).transpose(0, 3, 1, 2, 4)
        else:
            w = a["attn_w_o"][0][:, t[1] * P:(t[1] + 2) * P].reshape(4, P, 2, P).transpose(2, 0, 1, 3)
        w = w.reshape(-1, P, P)
        out[n, :, :len(w)] = w.transpose(1, 0, 2)
    return out.reshape(NT * P, TILE)


def lay_out_parameters(a):
    fm = lambda v: v.reshape(-1, P).T
    both = lambda v: np.concatenate([v, v], 1).T
    every = lambda v: np.broadcast_to(v.reshape(1, -1), (P, v.size))
    cc = np.stack([a["c_2"][0], a["c_ctx_2"]]).reshape(2, KC, P).transpose(2, 1, 0).reshape(P, -1)
    parts = {
        "norm": fm(a["norm_gain"]), "kv": fm(a["kv_norm_gain"]), "pscale": fm(a["pool_scale"]),
        "bada": fm(a["b_ada_2"]), "lng": fm(a["ln_g_2"]), "lnb": fm(a["ln_b_2"]), "cc": cc,
        "lb": fm(a["hg_lb_logits_2"]), "hgn": both(a["hg_norm_g_2"]), "gaq": both(a["ga_q_norm_g_2"]),
        "gak": both(a["ga_k_norm_g_2"]), "dfg": both(a["df_subln_g_2"]), "sink": every(a["wn_sink_2"]),
        "dfl": every(a["df_lambda_2"]),
    }
    return np.concatenate([parts[n] for n in PAR_WIDTHS], 1)


def dilated_units():
    units = []
    for i in range(LQ):
        for h in range(2):
            blocks = [(0, j, "g0diag" if j == i else "g0prev") for j in range(max(i - 1, 0), i + 1)]
            for g in (1, 2):
                blocks += [(g, j, f"g{g}diag" if j == i else f"g{g}off") for j in range(i + 1)]
            units.append((i, h, blocks))
    return units


def all_keys(i):
    return [(0, j, None) for j in (range(NQ) if i < LQ else range(LQ, NQ))]


def window_keys(i):
    near = [(0, j, {-1: "wprev", 0: None, 1: "wnext"}[j - i]) for j in range(i - 1, i + 2) if 0 <= j < LQ]
    return (near if i < LQ else []) + [(0, j, None) for j in range(LQ, NQ)]


class Tally:

    def __init__(self):
        self.n = {}

    def take(self, name, k=1):
        at = self.n.get(name, 0)
        self.n[name] = at + k
        return at

    def at(self, name):
        return self.n.get(name, 0)


WORK = 9728
CONST_LOADS = 4 + KC
MAGIC = 1.5 * 2.0 ** 23
C1, C2, C3 = 6.28125, 0.0019350051879882812, 3.0199159819567529e-07
PI_IN = 3.1415925


def build(nc, wts, par, con, tab, masks, levels, pos, x, ctx_in, out, scratch, stop=None):
    ctx = ExitStack()
    with ctx:
        def sb(name, shape, dt=F32):
            return ctx.enter_context(nc.sbuf_tensor(name, shape, dt))

        def sem(name):
            return ctx.enter_context(nc.semaphore(name))

        raw = sb("raw", [P, RAW, TILE])
        wh = sb("wh", [P, SPLIT, TILE], F32R)
        wl = sb("wl", [P, SPLIT, TILE], F32R)
        xh = sb("xh", [P, KC, TOK], F32R)
        xl = sb("xl", [P, KC, TOK], F32R)
        ah = sb("ah", [P, KC * TOK], F32R)
        al = sb("al", [P, KC * TOK], F32R)
        hc = sb("hc", [P, KC, TOK])
        tb = sb("tb", [P, NTAB])
        mk = sb("mk", [P, NMASK], BF16)
        lev = sb("lev", [P, 2, NLOW, BLK], BF16)
        pr = sb("pr", [P, NPAR])
        cn = sb("cn", [P, NCON])
        ada = sb("ada", [P, DEPTH, 24, 2])
        sm = sb("sm", [P, 128])
        work = sb("work", [P, WORK])
        ps = ctx.enter_context(nc.psum_tensor("ps", [P, 8, 512], F32))

        ada_all = ada[:, :, :, :].rearrange("p l m s -> p (l m) s")

        def col(name, i=0, n=1):
            return pr[:, PAR_AT[name] + i:PAR_AT[name] + i + n]

        def const(name, n=None):
            return cn[:, CON_AT[name]:CON_AT[name] + (n or CON_WIDTHS[name])]

        def mask(name):
            return mk[:, MASKS.index(name) * P:(MASKS.index(name) + 1) * P]

        ident, ones = const("ident"), const("ones")
        eps_c, ln_eps_c, one_c = sm[:, 0:1], sm[:, 1:2], sm[:, 2:3]
        mx, negm, den, rden = sm[:, 4:6], sm[:, 6:8], sm[:, 8:11], sm[:, 11:13]
        esink, lamc, lnlb, ln1lb = sm[:, 13:16], sm[:, 16:18], sm[:, 22:26], sm[:, 26:30]
        hs, sd = sm[:, 32:44], sm[:, 44:56]
        lt = sm[:, 64:96]

        def ahk(k, n=SEQ):
            return ah[:, k * n:(k + 1) * n]

        def alk(k, n=SEQ):
            return al[:, k * n:(k + 1) * n]

        def area(at, n):
            assert at + n <= WORK, (at, n)
            return work[:, at:at + n]

        fo = area(0, KC * SEQ).rearrange("p (k t) -> p k t", k=KC)
        sil = area(4096, 2 * SEQ).rearrange("p (s t) -> p s t", s=2)
        sq = area(5120, 2 * SEQ).rearrange("p (s t) -> p s t", s=2)
        tt = area(6144, 2 * SEQ).rearrange("p (s t) -> p s t", s=2)
        ada_rows = area(7168, 4 * FOUR)[0:2]
        pads = tb[:, 0:3 * (PAD + SEQ)].rearrange("p (s t) -> p s t", s=3)
        qk1 = area(0, 6 * SEQ).rearrange("p (s t) -> p s t", s=6)
        v1 = area(3072, 3 * SEQ).rearrange("p (g t) -> p g t", g=3)
        cs1 = tb[:, 0:2 * SEQ].rearrange("p (s t) -> p s t", s=2)
        t1 = tb[:, 2 * SEQ:4 * SEQ].rearrange("p (s t) -> p s t", s=2)

        const_in, cond_in = sem("const_in"), sem("cond_in")
        raw_in = [sem(f"raw_in{s}") for s in range(RAW)]
        hi_done, lo_done = sem("hi_done"), sem("lo_done")
        tile_done = sem("tile_done")
        taken = sem("taken")
        sil_ready, a_ready, x_ready, h_ready = sem("sil_ready"), sem("a_ready"), sem("x_ready"), sem("h_ready")
        part_ready, part_hi = sem("part_ready"), sem("part_hi")
        sq_ready, sq_used, rstd_ready = sem("sq_ready"), sem("sq_used"), sem("rstd_ready")
        act_own, dve_own = sem("act_own"), sem("dve_own")
        h0_out, h0_in = sem("h0_out"), sem("h0_in")
        d2p, d2a, a2d, a2p, p2d, p2a = (sem(n) for n in (
            "vector_to_tensor", "vector_to_scalar", "scalar_to_vector", "scalar_to_tensor",
            "tensor_to_vector", "tensor_to_scalar"))
        s_full, neg_ready, p_ready = sem("s_full"), sem("neg_ready"), sem("p_ready")
        pt_full, pt_act, pt_dve = sem("pt_full"), sem("pt_act"), sem("pt_dve")
        o_full, o_taken = sem("o_full"), sem("o_taken")
        stored = sem("stored")
        ada_done = sem("ada_done")
        ada_taken = sem("ada_taken")
        sums_ready = sem("sums_ready")
        dist_ready, decay_ready, ops_ready = sem("dist_ready"), sem("decay_ready"), sem("ops_ready")
        near_full, far_full, turned = sem("near_full"), sem("far_full"), sem("turned")
        near_ready, far_ready, kdt_ready = sem("near_ready"), sem("far_ready"), sem("kdt_ready")
        step_full, state_ready = sem("step_full"), sem("state_ready")
        block = ctx.enter_context(nc.Block())

        def runs(n):
            return [(0, HALF), (HALF, HALF)] if n == TOK else [(0, n)]

        def in_runs(v, n):
            return v[:, 0:n].rearrange("p (b t) -> p b t", b=len(runs(n)))

        def banks(b, n):
            return ps[:, b:b + len(runs(n)), 0:runs(n)[0][1]]

        def tokens(what, layer):
            return SEQ if layer == DEPTH - 1 and what in "qg" else TOK
        PHASES = [("ffn", 0, 0), ("pool",), ("ffn", 0, 1), ("keep",), ("ffn", 1, 0), ("dilated",), ("ffn", 1, 1)]
        for layer in range(DEPTH):
            PHASES += [("ada", layer), ("scan", layer, 0), ("scan", layer, 1), ("attend", layer, "global", 0),
                       ("attend", layer, "global", 1), ("attend", layer, "diff", 0), ("attend", layer, "diff", 1),
                       ("attend", layer, "window", 0), ("attend", layer, "window", 1), ("mix", layer)]
        PHASES = PHASES[:stop]
        H_TOTAL = KC * (1 + sum(p[0] in ("ffn", "pool", "dilated", "mix") for p in PHASES))

        q2, sg2, o2 = area(0, TOK), area(TOK, TOK), area(2 * TOK, TOK)
        ta, tbuf = area(3 * TOK, 512), area(3 * TOK + 512, 512)
        sq2 = area(3 * TOK, TOK)
        k2, v2 = area(3 * TOK + 1024, TOK), area(4 * TOK + 1024, TOK)
        P2AT = 5 * TOK + 1024
        fv1, fv2 = area(4608, SEQ), area(P2AT, TOK)
        sq_q, sz, sk, sv, sg, so, sz2 = (area(i * TOK, TOK) for i in range(7))
        se, sw = area(7 * TOK, TOK), area(8 * TOK, TOK)
        SX = 7 * TOK
        levels_of = [area(SX + i * LEVELS * P, LEVELS * P) for i in range(2)]
        SX += 2 * LEVELS * P
        qi = [area(SX + i * P, P) for i in range(3)]
        kd = [area(SX + (3 + i) * P, P) for i in range(2)]
        kdt = [area(SX + (5 + i) * P, P) for i in range(2)]
        state = area(SX + 7 * P, P)
        near = [area(SX + (8 + 2 * i) * P, 2 * P).rearrange("p (h t) -> p h t", h=2) for i in range(2)]
        far = [area(SX + (12 + 2 * i) * P, 2 * P).rearrange("p (h t) -> p h t", h=2) for i in range(2)]
        SX += 16 * P
        lowp = area(SX, 2 * NLOW * BLK).rearrange("p (h l t) -> p h l t", h=2, l=NLOW)
        lows = area(SX + 2 * NLOW * BLK, 2 * BLK).rearrange("p (h t) -> p h t", h=2)

        def level(s, l):
            return levels_of[s % 2][:, l * P:(l + 1) * P]

        def order(way):
            return [LQ, LQ + 1, 0, 1, 2, 3] if way == 0 else [5, 4, 3, 2, 1, 0]

        def has_output(t, layer):
            return t < out_tiles(layer)

        def attention(kind, layer=0):
            units = []
            if kind == "dilated":
                for i, h, blocks in dilated_units():
                    units.append(dict(i=i, part=HEAD * h, width=HEAD, blocks=blocks, h=h, add=False))
            else:
                for i in range(out_tiles(layer)):
                    for h in range(2):
                        keys = window_keys(i) if kind == "window" else all_keys(i)
                        for m in range(2 if kind == "diff" else 1):
                            w = HEAD // 2 if kind == "diff" else HEAD
                            units.append(dict(i=i, part=HEAD * h + w * m, width=w, blocks=keys, h=h, add=m == 1))
            return units

        def out_tiles(layer):
            return NQ if layer < DEPTH - 1 else LQ

        def buffers(kind):
            if kind == "dilated":
                q = lambda u, g: qk1[u["part"]:u["part"] + u["width"], 2 * g, u["i"] * P:(u["i"] + 1) * P]
                k = lambda u, g, j, n: qk1[u["part"]:u["part"] + u["width"], 2 * g + 1, j * P:(j + n) * P]
                v = lambda u, g, j: v1[:, g, j * P + HEAD * u["h"]:j * P + HEAD * (u["h"] + 1)]
                p = [area(4608 + 1280 * s, 1280) for s in range(2)]
                pt = [area(4608 + 1280 * (s + 2), 1280) for s in range(2)]
                o = t1.rearrange("p s t -> p (s t)")[:, 0:SEQ]
            else:
                q = lambda u, g: q2[u["part"]:u["part"] + u["width"], u["i"] * P:(u["i"] + 1) * P]
                k = lambda u, g, j, n: k2[u["part"]:u["part"] + u["width"], j * P:(j + n) * P]
                v = lambda u, g, j: v2[:, j * P + HEAD * u["h"]:j * P + HEAD * (u["h"] + 1)]
                p = [area(P2AT + TOK * s, TOK) for s in range(2)]
                pt = [area(P2AT + TOK * (s + 2), TOK) for s in range(2)]
                o = o2
            return q, k, v, p, pt, o

        def slot_at(i, unit):
            n = len(unit["blocks"]) * P
            return 2 * 512 if i % 2 == 0 else 7 * 512 - max(n, 1024)

        def key_runs(i, unit):
            runs_ = []
            for b, (g, j, _) in enumerate(unit["blocks"]):
                same_bank = (slot_at(i, unit) + b * P) % 512
                if b and same_bank and unit["blocks"][b - 1][:2] == (g, j - 1):
                    runs_[-1][1] += 1
                else:
                    runs_.append([b, 1])
            return runs_

        def slot(i, unit):
            n, at = len(unit["blocks"]) * P, slot_at(i, unit)
            return ps[:, :, :].rearrange("p b n -> p (b n)")[:, at:at + n]

        def over(unit):
            return len(unit["blocks"]) > 8

        def o_psum(i, kind):
            return ps[:, 7 if i % 2 or kind == "dilated" else 4, 0:HEAD]

        def groups(unit):
            n = len(unit["blocks"])
            return [range(a, min(a + 4, n)) for a in range(0, n, 4)]

        def pass_tiles(kind, hp):
            if kind == "diff":
                return "qkvg"
            if kind == "window" and hp == 1:
                return "gq"
            return "kvqg" if hp == 0 else "qg"

        def qk_parts(kind, hp):
            q, k = dict(diff=(6, 7), window=(6, 7)).get(kind, (4, 5))
            if kind == "window" and hp == 1:
                return xh[:, 0, :], xl[:, 0, :], ahk(k, TOK), alk(k, TOK)
            return ahk(q, TOK), alk(q, TOK), ahk(k, TOK), alk(k, TOK)

        def tiles_of(name, *rest):
            if name == "attend":
                return len(pass_tiles(*rest[1:]))
            if name == "ffn":
                return 2 * FC + len(FF_PARTS) * KC
            return dict(pool=2 * KC + 2, keep=0, dilated=9 * (A_HEADS // 2) + KC // 2, ada=0, scan=5, mix=KC)[name]

        def has_ada(layer, i):
            return (layer, i) in ADA_FFNS

        def halves(v, l):
            n = 1 << l
            v = v.rearrange("p (a c) -> p a c", c=2 * n)
            return v[:, :, 0:n], v[:, :, n:2 * n]

        def far_products(way):
            out_ = []
            for l, s0, q0, n in ((6, 0, 64, 64), (5, 0, 32, 32), (5, 64, 96, 32)):
                if way:
                    s0, q0 = q0, s0
                out_.append((slice(s0, s0 + n), slice(q0, q0 + n), l))
            return out_

        def hs_of(layer):
            return hs[:, 0:2 * out_tiles(layer)]

        def lnsq(k):
            return area(k % 2 * TOK, TOK)

        def x_parts(layer=None):
            n = SEQ if layer is None else TOK
            src = (lambda k: tt[:, k % 2, :]) if layer is None else (lambda k: area(k % 2 * TOK, TOK))
            return [(src(k), xh[:, k, 0:n], xl[:, k, 0:n]) for k in range(KC)]

        def kv_parts():
            return [(tt[:, k % 2, :], ahk(k), alk(k)) for k in range(KC)]

        @block.sync
        def _(sp):
            for n in range(RAW):
                sp.dma_start(raw[:, n, :], wts[n * P:(n + 1) * P, :]).then_inc(raw_in[n], 16)
            freed = {False: 0, True: 0}

            def load(n, src, slot_, i, per):
                ada = IS_ADA[n - RAW]
                sp.wait_ge(ada_done if ada else lo_done, i * per[ada] + (freed[ada] + 1))
                freed[ada] += 1
                sp.dma_start(raw[:, slot_, :], src).then_inc(raw_in[slot_], 16)

            b, blocks = 1, NT // RAW
            kinds = lambda b: IS_ADA[(b - 1) * RAW:b * RAW]
            while b < blocks:
                e = b + 1
                while e < blocks and kinds(e) == kinds(b):
                    e += 1
                per = {ada: kinds(b).count(ada) for ada in (False, True)}
                with turns(sp, e - b) as i:
                    for j in range(RAW):
                        load(b * RAW + j, wts[bass.ds((i * RAW + (b * RAW + j)) * P, P), :], j, i, per)
                for ada in per:
                    freed[ada] += per[ada] * (e - b - 1)
                b = e
            for n in range(blocks * RAW, NT):
                load(n, wts[n * P:(n + 1) * P, :], n % RAW, 0, per)
            for k in range(KC):
                sp.wait_ge(h_ready, H_TOTAL - KC + k + 1)
                sp.dma_start(out[k * P:(k + 1) * P, :], hc[:, k, 0:SEQ]).then_inc(stored, 16)
            sp.wait_ge(stored, 16 * KC)

        @block.gpsimd
        def _(pool):
            c = Tally()

            def remainder(n):
                pool.wait_ge(hi_done, n + 1)
                pool.tensor_tensor(wl[:, n % SPLIT, :], raw[:, LOADED[n] % RAW, :], wh[:, n % SPLIT, :].bitcast(F32),
                                   ALU.subtract).then_inc(lo_done, 1)

            def remainders(upto):
                n0 = c.at("tile")
                blocks = (upto - n0) // 4
                for b, times, _ in even_runs(n0, blocks):
                    with turns(pool, times) as i:
                        for j in range(4):
                            n = n0 + 4 * b + j
                            pool.wait_ge(hi_done, i * 4 + (n + 1))
                            pool.tensor_tensor(wl[:, n % SPLIT, :], raw[:, LOADED[n] % RAW, :], wh[:, n % SPLIT, :].bitcast(F32),
                                               ALU.subtract).then_inc(lo_done, 1)
                for n in range(n0 + 4 * blocks, upto):
                    remainder(n)
                c.n["tile"] = upto

            def scan(layer, hp):
                for way in range(2):
                    c.take("way")
                    pool.wait_ge(sums_ready, c.at("way"))
                    for t in order(way):
                        s = c.take("scan tile")
                        if not has_output(t, layer):
                            continue
                        if s >= 2:
                            pool.wait_ge(turned, s - 1)
                        zb = sz[:, t * P:(t + 1) * P]
                        for l in range(LEVELS):
                            n = 1 << l
                            v, w = (x_.rearrange("p (a c) -> p a c", c=2 * n) for x_ in (zb, level(s, l)))
                            border = v[:, :, n - 1 + way:n + way].to_broadcast([P, P // (2 * n), 2 * n])
                            ins = pool.tensor_tensor(w, v, border, ALU.subtract)
                        ins.then_inc(dist_ready, 1)

            def low_parts(parts, ready):
                for src, hi, lo in parts:
                    pool.wait_ge(part_hi, c.take("part") + 1)
                    pool.tensor_tensor(lo, src, hi.bitcast(F32), ALU.subtract).then_inc(ready, 1)

            used = 2
            for name, *rest in PHASES:
                if name in ("ffn", "pool", "dilated", "ada"):
                    remainders(used)
                    low_parts(x_parts(rest[0] if name == "ada" else None), x_ready)
                if name == "dilated":
                    low_parts(kv_parts(), a_ready)
                used += tiles_of(name, *rest)
                if name == "scan":
                    remainders(min(used, NS))
                    scan(*rest)
            remainders(NS)

        @block.scalar
        def _(act):
            c = Tally()

            def own(ins):
                c.take("own")
                ins.then_inc(act_own, 1)
                act.wait_ge(act_own, c.at("own"))

            def give(ins, s, name):
                c.take(name)
                ins.then_inc(s, 1)

            def get(s, name, k=1):
                c.take(name, k)
                act.wait_ge(s, c.at(name))

            def hi(n):
                if n < NS:
                    at = LOADED[n]
                    act.wait_ge(raw_in[at % RAW], 16 * (at // RAW + 1))
                    act.activation(wh[:, n % SPLIT, :], raw[:, at % RAW, :], ACT.Copy).then_inc(hi_done, 1)

            def tile():
                n = c.take("tile")
                act.wait_ge(tile_done, n + 1)
                hi(n + 2)
                return n

            def tiles_loop(k):
                n0 = c.take("tile", k)
                loop_tiles(n0, k // 4, lambda i, n, j: None)

            def loop_tiles(n0, blocks, after):
                for b, times, step in even_runs(n0 + 2, blocks):
                    with turns(act, times) as i:
                        for j in range(4):
                            n = n0 + 4 * b + j
                            at = LOADED[n + 2]
                            act.wait_ge(tile_done, i * 4 + (n + 1))
                            act.wait_ge(raw_in[at % RAW], i * (16 * step // RAW) + 16 * (at // RAW + 1))
                            act.activation(wh[:, n % SPLIT, :], raw[:, at % RAW, :], ACT.Copy).then_inc(hi_done, 1)
                            after(i, n, j)

            def exp_ln_tables():
                act.preload_act_table_set("natural_log_exp_and_others")

            def square(src):
                n = c.take("sq")
                if n >= 2:
                    act.wait_ge(sq_used, n - 1)
                act.activation(sq[:, n % 2, :], src, ACT.Square).then_inc(sq_ready, 1)

            def rstd(bank, scale=1.0 / D, bias=None):
                own(act.activation(bank, bank, ACT.Ln, bias=bias if bias is not None else eps_c, scale=scale))
                act.activation(bank, bank, ACT.Exp, scale=-0.5).then_inc(rstd_ready, 1)

            def norm_bank():
                return ps[:, 4 + c.take("norm") % 2, :]

            def norm(sem_, at, src):
                for k in range(KC):
                    act.wait_ge(sem_, at(k))
                    square(src(k))
                act.wait_ge(sq_used, c.at("sq"))
                rstd(norm_bank())

            def high_parts(parts):
                for src, hi, lo in parts:
                    act.wait_ge(part_ready, c.take("part") + 1)
                    act.activation(hi, src, ACT.Copy).then_inc(part_hi, 1)

            def h_squares():
                base = c.at("h")
                norm(h_ready, lambda k: base + k + 1, lambda k: hc[:, k, 0:SEQ])
                high_parts(x_parts())

            def f_squares():
                n = c.at("tile")
                norm(taken, lambda k: n - KC + k + 1 + 4, lambda k: fo[:, k, :])

            def ffn(layer, i):
                h_squares()
                for part in FF_PARTS:
                    def silu(i, n, j):
                        if j % 2 == 0:
                            act.wait_ge(taken, i * 4 + (n + 1))
                            act.activation(sil[:, j // 2, :], ps[:, n % 4, :], ACT.Silu).then_inc(sil_ready, 1)
                    n0 = c.take("tile", 2 * part)
                    loop_tiles(n0, part // 2, silu)
                    if part != FF_PARTS[-1]:
                        tiles_loop(KC)
                exp_ln_tables()
                for m in range(KC):
                    tile()
                    if m:
                        act.wait_ge(taken, c.at("tile") - 1 + 4)
                        square(fo[:, m - 1, :])
                act.wait_ge(taken, c.at("tile") + 4)
                square(fo[:, KC - 1, :])
                act.wait_ge(sq_used, c.at("sq"))
                rstd(norm_bank())
                c.take("h", KC)

            def pool():
                h_squares()
                tiles_loop(KC)
                tile(), tile()
                tiles_loop(KC)
                f_squares()
                c.take("h", KC)

            def keep():
                act.wait_ge(h_ready, c.at("h") + KC)
                act.dma_start(scratch, hc[:, :, 0:SEQ]).then_inc(h0_out, 16)

            def attend(kind, scale, sink=None, layer=0):
                units = attention(kind, layer)
                q, k, v, p, pt, o = buffers(kind)
                u0, g0 = c.at("unit"), c.at("group")
                ends = []
                for u in units:
                    ends.append(g0 + len(groups(u)) + (ends[-1] - g0 if ends else 0))

                def evacuate(i):
                    for b, blocks in enumerate(groups(units[i])):
                        c.take("group")
                        if b % 2 == 0:
                            act.wait_ge(pt_full, c.at("group"))
                            if i >= 2:
                                act.wait_ge(o_full, u0 + i - 1)
                            n = len(blocks) * P
                            act.activation(pt[i % 2][:, blocks[0] * P:blocks[0] * P + n],
                                           ps[:, (c.at("group") - 1) % 2, 0:n], ACT.Copy).then_inc(pt_act, 1)

                for i, u in enumerate(units):
                    n = len(u["blocks"]) * P
                    act.wait_ge(neg_ready, u0 + i + 1)
                    if i >= len(p):
                        act.wait_ge(pt_full, ends[i - len(p)])
                    if sink is not None:
                        own(act.activation(esink[:, i % 3:i % 3 + 1], sink(u), ACT.Exp, bias=negm[:, i % 2:i % 2 + 1]))
                    act.activation(p[i % len(p)][:, 0:n], slot(i, u), ACT.Exp, bias=negm[:, i % 2:i % 2 + 1],
                                   scale=scale, accum_out=den[:, i % 3:i % 3 + 1]).then_inc(p_ready, 1)
                    if i >= 1:
                        evacuate(i - 1)
                evacuate(len(units) - 1)
                c.take("unit", len(units))

            def dilated():
                h_squares()
                act.dma_start(t1[:, 1, :].bitcast(I32), pos).then_inc(cond_in, 16)
                act.wait_ge(h0_out, 16)
                act.dma_start(fo, scratch).then_inc(h0_in, 16)
                for s in range(2):
                    get(d2a, "d2a")
                    give(act.activation(cs1[:, s, :], t1[:, 0, :], ACT.Sin), a2d, "a2d")
                exp_ln_tables()
                norm(h0_in, lambda k: 16, lambda k: fo[:, k, :])
                high_parts(kv_parts())
                for hp in range(A_HEADS // 2):
                    for j in range(9):
                        tile()
                    attend("dilated", HEAD ** -0.5)
                for m in range(0, KC, 2):
                    tile()
                n = c.at("tile")
                norm(taken, lambda k: n - 4 + k // 2 + 1 + 4, lambda k: fo[:, k, :])
                act.dma_start(tb[:, :], tab).then_inc(cond_in, 16)
                c.take("h", KC)

            def nsp(e):
                own(act.activation(e, e, ACT.Exp, scale=-1.0))
                give(act.activation(e, e, ACT.Ln, bias=one_c), a2d, "a2d")

            def ada_phase(layer):
                high_parts(x_parts(layer))
                if layer == 0:
                    get(d2a, "d2a")
                    nsp(lt[:, 8:12])
                    get(d2a, "d2a")
                    give(act.activation(lt[:, 16:16 + 2 * DEPTH], lt[:, 16:16 + 2 * DEPTH], ACT.Exp), a2d, "a2d")

            def decays(s, t, way, layer):
                if s >= 3:
                    act.wait_ge(step_full, s - 2)
                if s >= 2:
                    act.wait_ge(turned, s - 1)
                b = sz[:, t * P:(t + 1) * P]
                last = t * P + (P - 1 if way == 0 else 0)
                act.activation(qi[s % 3], b, ACT.Exp)
                ins = act.activation(kd[s % 2], b, ACT.Exp, scale=-1.0, bias=sz[:, last:last + 1])
                if has_output(t, layer):
                    act.wait_ge(dist_ready, c.take("dist") + 1)
                    own(act.activation(levels_of[s % 2], levels_of[s % 2], ACT.Abs))
                    ins = act.activation(levels_of[s % 2], levels_of[s % 2], ACT.Exp, scale=-1.0)
                ins.then_inc(decay_ready, 1)

            def forget(layer, hp, way):
                get(d2a, "d2a")
                nsp(se)
                get(d2a, "d2a")
                give(act.activation(sk, sk, ACT.Exp, bias=0.0 if layer == 0 else ln1lb[:, way * 2 + hp:way * 2 + hp + 1]), a2d, "a2d")
                if layer:
                    get(d2a, "d2a")
                    nsp(se)

            def scan(layer, hp):
                for j, what in enumerate("qgfif"):
                    n = tile()
                    if what in "qg":
                        v = (sq_q if what == "q" else sg)[:, 0:tokens(what, layer)]
                        act.wait_ge(taken, n + 1 + 4)
                        give(act.activation(v, v, ACT.Silu), a2d, "a2d")
                    if j == 2:
                        exp_ln_tables()
                        forget(layer, hp, 0)
                for way in range(2):
                    if way:
                        forget(layer, hp, 1)
                    c.take("way")
                    act.wait_ge(sums_ready, c.at("way"))
                    s0 = c.take("scan tile", NQ)
                    tiles_ = order(way)
                    for i in range(-1, NQ):
                        if i + 1 < NQ:
                            decays(s0 + i + 1, tiles_[i + 1], way, layer)
                        if i >= 0 and has_output(tiles_[i], layer):
                            n = c.take("full")
                            act.wait_ge(far_full, n + 1)
                            if n >= 2:
                                act.wait_ge(step_full, s0 + i - 1)
                            for rows, cols, l in far_products(way):
                                ins = act.activation(far[n % 2][rows, :, cols], ps[rows, 6:8, cols.start:cols.stop], ACT.Copy)
                            ins.then_inc(far_ready, 1)
                get(d2a, "d2a")
                own(act.activation(hs_of(layer), hs_of(layer), ACT.Ln, bias=eps_c, scale=1.0 / HEAD))
                give(act.activation(hs_of(layer), hs_of(layer), ACT.Exp, scale=-0.5), a2d, "a2d")

            def head_norm(v, n_tok):
                get(d2a, "d2a")
                give(act.activation(sq2[:, 0:n_tok], v[:, 0:n_tok], ACT.Square), a2p, "a2p")
                get(p2a, "p2a")
                b = banks(6, n_tok)
                own(act.activation(b, b, ACT.Ln, bias=eps_c, scale=1.0 / HEAD))
                give(act.activation(b, b, ACT.Exp, scale=-0.5), a2d, "a2d")

            def attend_phase(layer, kind, hp):
                for what in pass_tiles(kind, hp):
                    n = tile()
                    if what == "g":
                        act.wait_ge(taken, n + 1 + 4)
                        v = sg2[:, 0:tokens(what, layer)]
                        give(act.activation(v, v, ACT.Silu), a2d, "a2d")
                        exp_ln_tables()
                    if what in "qk" and kind == "global":
                        head_norm(q2 if what == "q" else k2, tokens(what, layer))
                if kind == "window":
                    attend(kind, HEAD ** -0.5, lambda u: col("sink", layer * 4 + 2 * u["h"] + hp), layer=layer)
                else:
                    attend(kind, (HEAD // 2 if kind == "diff" else HEAD) ** -0.5, layer=layer)
                if kind == "diff":
                    get(d2a, "d2a")
                    own(act.activation(hs_of(layer), hs_of(layer), ACT.Ln, bias=eps_c, scale=1.0 / HEAD))
                    give(act.activation(hs_of(layer), hs_of(layer), ACT.Exp, scale=-0.5), a2d, "a2d")

            def mix(layer):
                for m in range(KC):
                    tile()
                for k in range(KC):
                    get(d2a, "d2a")
                    if k >= 2:
                        get(p2a, "p2a")
                    n_tok = out_tiles(layer) * P
                    give(act.activation(lnsq(k)[:, 0:n_tok], hc[:, k, 0:n_tok], ACT.Square), a2p, "a2p")
                get(p2a, "p2a", 2)
                b = banks(6, n_tok)
                own(act.activation(b, b, ACT.Ln, bias=ln_eps_c, scale=1.0 / D))
                give(act.activation(b, b, ACT.Exp, scale=-0.5), a2d, "a2d")
                c.take("h", KC)

            for dst, src in ((cn[:], con), (pr[:], par), (area(0, NMASK), masks), (area(NMASK, NLEV), levels)):
                act.dma_start(dst, src).then_inc(const_in, 16)
            for k in range(KC):
                act.dma_start(hc[:, k, 0:SEQ], x[k * P:(k + 1) * P, :]).then_inc(const_in, 16)
            act.dma_start(hc[:, :, SEQ:TOK], ctx_in).then_inc(cond_in, 16)
            act.wait_ge(const_in, CONST_LOADS * 16)
            give(act.activation(col("cc", 0, 2 * KC), col("cc", 0, 2 * KC), ACT.Silu), a2p, "a2p")
            exp_ln_tables()
            hi(0), hi(1)
            run = dict(ffn=ffn, pool=pool, keep=keep, dilated=dilated, ada=ada_phase, scan=scan, attend=attend_phase, mix=mix)
            for name, *rest in PHASES:
                run[name](*rest)

        @block.tensor
        def _(pe):
            c = Tally()

            def give(ins, s, name):
                c.take(name)
                ins.then_inc(s, 1)

            def get(s, name, k=1):
                c.take(name, k)
                pe.wait_ge(s, c.at(name))

            def mm3(outs, s, k, hi, lo, cols, start, stop):
                for w, x_, first, last in ((wh, hi, start, False), (wh, lo, False, False), (wl, hi, False, stop)):
                    for out_, at in zip(outs, cols):
                        ins = pe.matmul(out_, w[:, s, k * P:(k + 1) * P], x_(k, at), start=first, stop=last)
                return ins

            def settle():
                if c.at("tile"):
                    pe.wait_ge(taken, c.at("tile") + 4)

            def tiles_loop(n0, times, kn, hi, lo):
                with pe.Fori(0, times) as i:
                    for j in range(4):
                        pe.wait_ge(lo_done, i * 4 + (n0 + j + 1))
                        pe.wait_ge(taken, i * 4 + (n0 + j + 1))
                        for k in range(kn):
                            ins = mm3([ps[:, (n0 + j) % 4, 0:SEQ]], (n0 + j) % SPLIT, k, hi, lo, [0], k == 0, k == kn - 1)
                        ins.then_inc(tile_done, 1)

            def chunks(k, kn, hi, lo):
                tiles_loop(c.take("tile", k // 4 * 4), k // 4, kn, hi, lo)
                for j in range(k % 4):
                    n = tile()
                    pe.wait_ge(taken, n + 1)
                    for kk in range(kn):
                        ins = mm3([ps[:, n % 4, 0:SEQ]], n % SPLIT, kk, hi, lo, [0], kk == 0, kk == kn - 1)
                    ins.then_inc(tile_done, 1)

            def tile():
                n = c.take("tile")
                pe.wait_ge(lo_done, n + 1)
                return n

            def pair():
                n = tile()
                pe.wait_ge(taken, n + 3)
                return n, [2 * (n % 2), 2 * (n % 2) + 1]

            def down_and_ada(part):
                n0, g0 = c.take("tile", KC), c.take("ada group", KC // 4)
                with pe.Fori(0, KC // 4) as i:
                    for j in range(4):
                        n, at = n0 + j, LOADED[n0 + j] + 1
                        pe.wait_ge(lo_done, i * 4 + (n + 1))
                        pe.wait_ge(taken, i * 4 + (n + 1))
                        for k in range(part):
                            ins = mm3([ps[:, n % 4, 0:SEQ]], n % SPLIT, k, a_hi, a_lo, [0], k == 0, k == part - 1)
                        ins.then_inc(tile_done, 1)
                        pe.wait_ge(raw_in[at % RAW], i * 32 + 16 * (at // RAW + 1))
                        if j == 0:
                            pe.wait_ge(ada_taken, i + (g0 + 1))
                        for k in range(2):
                            ins = pe.matmul(ps[0:2, 6, :], col("cc", 2 * (2 * j + k), 2), raw[:, at % RAW, k * FOUR:(k + 1) * FOUR],
                                            start=j == 0 and k == 0, stop=j == 3 and k == 1)
                        ins.then_inc(ada_done, 1)

            def turn_ada():
                pe.wait_ge(ada_taken, c.at("ada group") + 1)
                for m in range(16):
                    ins = pe.matmul(ps[:, 7, 2 * m:2 * m + 2], ada_rows[:, m * P:(m + 1) * P], const("ident", 2)[0:2, :], start=True, stop=True)
                give(ins, p2d, "p2d")

            x_hi = lambda k, at: xh[:, k, 0:SEQ]
            x_lo = lambda k, at: xl[:, k, 0:SEQ]
            a_hi = lambda k, at: ahk(k)
            a_lo = lambda k, at: alk(k)

            def add_squares(k):
                n = c.take("sq")
                if k == 0:
                    c.take("norm")
                pe.wait_ge(sq_ready, n + 1)
                pe.matmul(ps[:, 4 + (c.at("norm") - 1) % 2, :], ones, sq[:, n % 2, :],
                          start=k == 0, stop=k == KC - 1).then_inc(sq_used, 1)

            def norm():
                for k in range(KC):
                    add_squares(k)

            def wait_x():
                c.take("x", KC)
                pe.wait_ge(x_ready, c.at("x"))

            def first_two(tiles):
                n0, x0 = c.take("tile", 2), c.take("x", KC)
                pe.wait_ge(lo_done, n0 + 2)
                for k in range(KC):
                    pe.wait_ge(x_ready, x0 + k + 1)
                    for j, (bb, rr) in enumerate(tiles):
                        ins = mm3([ps[:, b, 0:w] for b, (_, w) in zip(bb, rr)], (n0 + j) % SPLIT, k, m_hi, m_lo, rr, k == 0, k == KC - 1)
                        if k == KC - 1:
                            ins.then_inc(tile_done, 1)

            def first_two_chunks():
                n = c.at("tile")
                first_two([([(n + j) % 4], [(0, SEQ)]) for j in range(2)])

            def wait_a(k):
                c.take("a", k)
                pe.wait_ge(a_ready, c.at("a"))

            def ffn(layer, i):
                norm()
                settle()
                first_two_chunks()
                for number, part in enumerate(FF_PARTS):
                    chunks(2 * part - (2 if number == 0 else 0), KC, x_hi, x_lo)
                    wait_a(part)
                    if part != FF_PARTS[-1]:
                        if has_ada(layer, i):
                            down_and_ada(part)
                        else:
                            chunks(KC, part, a_hi, a_lo)
                for m in range(KC):
                    n = tile()
                    pe.wait_ge(taken, n + 1)
                    for k in range(part):
                        ins = mm3([ps[:, n % 4, :]], n % SPLIT, k, a_hi, a_lo, [0], k == 0, k == part - 1)
                    ins.then_inc(tile_done, 1)
                    if m:
                        add_squares(m - 1)
                add_squares(KC - 1)
                if has_ada(layer, i):
                    turn_ada()

            def pool():
                norm()
                settle()
                first_two_chunks()
                chunks(KC - 2, KC, x_hi, x_lo)
                wait_a(KC)
                for g2 in range(2):
                    n = tile()
                    settle_but_this(n)
                    for b in range(4):
                        g, m = 2 * g2 + b // 2, b % 2
                        for k in range(2):
                            blk = (b // 2) * 4 + m * 2 + k
                            for w, x_, first, last in ((wh, a_hi, k == 0, False), (wh, a_lo, False, False), (wl, a_hi, False, k == 1)):
                                ins = pe.matmul(ps[:, b, :], w[:, n % SPLIT, blk * P:(blk + 1) * P], x_(2 * g + k, 0), start=first, stop=last)
                    ins.then_inc(tile_done, 1)
                wait_x()
                settle()
                chunks(KC, KC, x_hi, x_lo)
                norm()

            def settle_but_this(n):
                pe.wait_ge(taken, n + 4)

            def attend(kind, layer=0, parts=None):
                units = attention(kind, layer)
                q, k, v, p, pt, o = buffers(kind)
                u0 = c.at("unit")
                evacuated = c.n.setdefault("evacuated", [])

                def scores(i):
                    u = units[i]
                    if i >= 2:
                        pe.wait_ge(p_ready, u0 + i - 1)
                    if i >= 1 and over(u) and over(units[i - 1]):
                        pe.wait_ge(p_ready, u0 + i)
                    for b, n in key_runs(i, u):
                        g, j, _ = u["blocks"][b]
                        masked = [a for a in range(b, b + n) if u["blocks"][a][2] is not None]
                        out_ = slot(i, u)[:, b * P:(b + n) * P]
                        if parts is None:
                            pairs = [(q(u, g), k(u, g, j, n))]
                        else:
                            qh, ql, kh, kl = parts
                            of = lambda v, at, w: v[u["part"]:u["part"] + u["width"], at * P:(at + w) * P]
                            pairs = [(of(a_, u["i"], 1), of(b_, j, n)) for a_, b_ in ((qh, kh), (qh, kl), (ql, kh))]
                        for a, (qq, kk) in enumerate(pairs):
                            ins = pe.matmul(out_, qq, kk, start=a == 0, stop=a == len(pairs) - 1 and not masked, skip_group_check=True)
                        for a in masked:
                            ins = pe.matmul(slot(i, u)[:, a * P:(a + 1) * P], mask("ident"), mask(u["blocks"][a][2]),
                                            start=False, stop=a == masked[-1], skip_group_check=True)
                    ins.then_inc(s_full, 1)

                def transposes(i):
                    u = units[i]
                    pe.wait_ge(p_ready, u0 + i + 1)
                    for b, blocks in enumerate(groups(u)):
                        g = c.take("group")
                        name = "pt_act" if b % 2 == 0 else "pt_dve"
                        if len(evacuated) >= 2:
                            s, count = evacuated[-2]
                            pe.wait_ge(pt_act if s == "pt_act" else pt_dve, count)
                        c.take(name)
                        evacuated.append((name, c.at(name)))
                        for a, blk in enumerate(blocks):
                            ins = pe.transpose(ps[:, g % 2, a * P:(a + 1) * P], p[i % len(p)][:, blk * P:(blk + 1) * P], ident)
                        ins.then_inc(pt_full, 1)

                def values(i, last_group):
                    u = units[i]
                    for s, count in evacuated[last_group - len(groups(u)):last_group]:
                        pe.wait_ge(pt_act if s == "pt_act" else pt_dve, count)
                    back = 1 if kind == "dilated" else 2
                    if i >= back:
                        pe.wait_ge(o_taken, u0 + i - back + 1)
                    n = len(u["blocks"])
                    for b, (g, j, m) in enumerate(u["blocks"]):
                        ins = pe.matmul(o_psum(i, kind), pt[i % 2][:, b * P:(b + 1) * P], v(u, g, j), start=b == 0, stop=b == n - 1)
                    ins.then_inc(o_full, 1)

                scores(0)
                ends = []
                for i in range(len(units)):
                    if i + 1 < len(units):
                        scores(i + 1)
                    transposes(i)
                    ends.append(len(evacuated))
                    if i >= 1:
                        values(i - 1, ends[i - 1])
                values(len(units) - 1, ends[-1])
                c.take("unit", len(units))

            def rotate(src, matrix):
                n = c.take("rot")
                give(pe.matmul(ps[:, 6 + n % 2, :], matrix, src, start=True, stop=True), p2d, "p2d")

            def turn_outputs(o, tiles, banks):
                for i in range(tiles):
                    at = (i % (tiles // len(banks))) * P
                    ins = pe.transpose(ps[:, banks[i // (tiles // len(banks))], at:at + P], o[:, i * P:(i + 1) * P], ident)
                give(ins, p2d, "p2d")

            def turn_values(src, tiles, banks):
                get(d2p, "d2p")
                turn_outputs(src, tiles, banks)

            def dilated():
                norm()
                norm()
                wait_x()
                wait_a(KC)
                for hp in range(A_HEADS // 2):
                    settle()
                    for g in range(3):
                        for what in range(3):
                            n = tile()
                            pe.wait_ge(taken, n + 1)
                            hi, lo = (x_hi, x_lo) if what == 0 else (a_hi, a_lo)
                            for k in range(KC):
                                ins = mm3([ps[:, n % 4, :]], n % SPLIT, k, hi, lo, [0], k == 0, k == KC - 1)
                            ins.then_inc(tile_done, 1)
                            if what == 0 and g:
                                turn_values(fv1, LQ, [5])
                            if what:
                                pe.wait_ge(taken, n + 4)
                                rotate(qk1[:, 2 * g + what - 1, :], const("rot32"))
                    turn_values(fv1, LQ, [5])
                    get(d2p, "d2p")
                    settle()
                    attend("dilated")
                    get(d2p, "d2p")
                    turn_outputs(buffers("dilated")[5], LQ, [4])
                wait_a(A_HEADS // 2)
                for m in range(0, KC, 2):
                    n, bb = pair()
                    for b in range(2):
                        for k in range(4):
                            blk = b * 4 + k
                            for w, x_, first, last in ((wh, ah, k == 0, False), (wh, al, False, False), (wl, ah, False, k == 3)):
                                ins = pe.matmul(ps[:, bb[b], :], w[:, n % SPLIT, blk * P:(blk + 1) * P],
                                                x_[:, (KC + k) * SEQ:(KC + k + 1) * SEQ], start=first, stop=last)
                    ins.then_inc(tile_done, 1)
                norm()

            def wide(hi, lo, n_tok=TOK):
                n, bb = pair()
                for k in range(KC):
                    ins = mm3([ps[:, b, 0:w] for b, (_, w) in zip(bb, runs(n_tok))], n % SPLIT, k, hi, lo,
                              runs(n_tok), k == 0, k == KC - 1)
                ins.then_inc(tile_done, 1)
                return n

            m_hi = lambda k, run: xh[:, k, run[0]:run[0] + run[1]]
            m_lo = lambda k, run: xl[:, k, run[0]:run[0] + run[1]]

            def products(s, t, way, full):
                pe.wait_ge(ops_ready, s + 1)
                if full:
                    n = c.take("full")
                    if n:
                        pe.wait_ge(near_ready, n)
                    for h in range(2):
                        r = slice(HEAD * h, HEAD * (h + 1))
                        for l in range(NLOW):
                            for b in range(P // BLK):
                                g = slice(t * P + b * BLK, t * P + (b + 1) * BLK)
                                kk, qq = sk[r, g], sq_q[r, g]
                                if l:
                                    kk = qq = level(s, l - 1)[r, b * BLK:(b + 1) * BLK]
                                ins = pe.matmul(ps[b * BLK:(b + 1) * BLK, 4 + h, l * BLK:(l + 1) * BLK], kk, qq, start=True, stop=True)
                    ins.then_inc(near_full, 1)
                    if n:
                        pe.wait_ge(far_ready, n)
                    for h in range(2):
                        r = slice(HEAD * h, HEAD * (h + 1))
                        for rows, cols, l in far_products(way):
                            ins = pe.matmul(ps[rows, 6 + h, cols], level(s, l)[r, rows], level(s, l)[r, cols], start=True, stop=True)
                    ins.then_inc(far_full, 1)
                if s:
                    pe.wait_ge(kdt_ready, s)
                pe.transpose(ps[:, 2, 0:P], kd[s % 2], ident).then_inc(turned, 1)

            def step(s, t, full):
                pe.wait_ge(kdt_ready, s + 1)
                pe.wait_ge(state_ready, s + c.at("way"))
                if full:
                    n = c.take("stepped")
                    pe.wait_ge(near_ready, n + 1)
                    pe.wait_ge(far_ready, n + 1)
                    pe.matmul(ps[:, n % 2, 0:P], qi[s % 3], state, start=True, stop=False, skip_group_check=True)
                    for h in range(2):
                        vv = sv[:, t * P + h * HEAD:t * P + (h + 1) * HEAD]
                        oo = ps[:, n % 2, h * HEAD:(h + 1) * HEAD]
                        pe.matmul(oo, near[n % 2][:, h, :], vv, start=False, stop=False, skip_group_check=True)
                        pe.matmul(oo, far[n % 2][:, h, :], vv, start=False, stop=h == 1, skip_group_check=True)
                pe.matmul(ps[:, 3, 0:P], kdt[s % 2], sv[:, t * P:(t + 1) * P], start=True, stop=True).then_inc(step_full, 1)

            def scan(layer, hp):
                if hp == 0:
                    settle()
                    n = c.at("tile")
                    first_two([([2 * ((n + j) % 2), 2 * ((n + j) % 2) + 1], runs(tokens(what, layer))) for j, what in enumerate("qg")])
                for j, what in enumerate("qgfif"):
                    if hp or j >= 2:
                        wide(m_hi, m_lo, tokens(what, layer))
                    if j == 4:
                        turn_values(so, NQ, [6, 7])
                settle()
                for way in range(2):
                    s0 = c.take("scan tile", NQ)
                    tiles_ = order(way)
                    c.take("way")
                    for i in range(-1, NQ):
                        if i + 1 < NQ:
                            products(s0 + i + 1, tiles_[i + 1], way, has_output(tiles_[i + 1], layer))
                        if i >= 0:
                            step(s0 + i, tiles_[i], has_output(tiles_[i], layer))
                get(d2p, "d2p")
                turn_outputs(so, out_tiles(layer), [6, 7][:len(runs(out_tiles(layer) * P))])

            def attend_phase(layer, kind, hp):
                last = None
                for what in pass_tiles(kind, hp):
                    wide(m_hi, m_lo, tokens(what, layer))
                    if last == "v":
                        turn_values(fv2, NQ, [6, 7])
                    last = what
                    if what in "qk":
                        n_tok = tokens(what, layer)
                        dst = q2 if what == "q" else k2
                        if kind == "global":
                            get(a2p, "a2p")
                            for b, (at, w) in enumerate(runs(n_tok)):
                                ins = pe.matmul(ps[:, 6 + b, 0:w], const("blk"), sq2[:, at:at + w], start=True, stop=True)
                            give(ins, p2a, "p2a")
                        get(d2p, "d2p")
                        give(pe.matmul(ps[:, 5, :], const("rot8" if kind == "diff" else "rot16"), dst[:, 0:SEQ], start=True, stop=True), p2d, "p2d")
                settle()
                get(d2p, "d2p")
                attend(kind, layer, qk_parts(kind, hp))
                get(d2p, "d2p")
                turn_outputs(o2, out_tiles(layer), [6, 7][:len(runs(out_tiles(layer) * P))])

            def mix(layer):
                wait_a(KC)
                settle()
                n_tok = out_tiles(layer) * P
                y_hi = lambda k, run: ah[:, k * TOK + run[0]:k * TOK + run[0] + run[1]]
                y_lo = lambda k, run: al[:, k * TOK + run[0]:k * TOK + run[0] + run[1]]
                for m in range(KC):
                    wide(y_hi, y_lo, n_tok)
                for k in range(KC):
                    get(d2p, "d2p")
                    for b, (at, w) in enumerate(runs(n_tok)):
                        ins = pe.matmul(ps[:, 4 + b, 0:w], ones, hc[:, k, at:at + w], start=k == 0, stop=k == KC - 1)
                give(ins, p2d, "p2d")
                for k in range(KC):
                    get(a2p, "a2p")
                    for b, (at, w) in enumerate(runs(n_tok)):
                        ins = pe.matmul(ps[:, 6 + b, 0:w], ones, lnsq(k)[:, at:at + w], start=k == 0, stop=k == KC - 1)
                    give(ins, p2a, "p2a")

            pe.wait_ge(const_in, CONST_LOADS * 16)
            get(a2p, "a2p")
            run = dict(ffn=ffn, pool=pool, keep=lambda: None, dilated=dilated, ada=lambda layer: None, scan=scan, attend=attend_phase, mix=mix)
            for name, *rest in PHASES:
                run[name](*rest)

        @block.vector
        def _(dve):
            c = Tally()

            def own(ins):
                c.take("own")
                ins.then_inc(dve_own, 1)
                dve.wait_ge(dve_own, c.at("own"))

            def give(ins, s, name):
                c.take(name)
                ins.then_inc(s, 1)
                dve.wait_ge(s, c.at(name))

            def signal(s, name):
                c.take(name)
                dve.sem_inc(s, 1)

            def get(s, name, k=1):
                c.take(name, k)
                dve.wait_ge(s, c.at(name))

            def tile():
                n = c.take("tile")
                dve.wait_ge(tile_done, n + 1)
                return n

            def took(ins, n):
                ins.then_inc(taken, 1)
                dve.wait_ge(taken, n + 5)

            def split(src, hi, lo, s, name):
                own(dve.tensor_copy(hi, src))
                give(dve.tensor_tensor(lo, src, hi.bitcast(F32), ALU.subtract), s, name)

            def rstd():
                n = c.take("norm")
                dve.wait_ge(rstd_ready, c.take("rstd") + 1)
                return ps[:, 4 + n % 2, :]

            def to_parts(parts, ready, name, form):
                x0 = c.take(name, KC)
                for k, (t, hi, lo) in enumerate(parts):
                    if k >= 2:
                        dve.wait_ge(ready, x0 + k - 1)
                    form(k, t).then_inc(part_ready, 1)

            def normalised(src, gain):
                r = rstd()
                return lambda k, t: dve.scalar_tensor_tensor(t, src(k), gain(k), r, ALU.mult, ALU.mult)

            def x_from_h(gain):
                to_parts(x_parts(), x_ready, "x", normalised(lambda k: hc[:, k, 0:SEQ], gain))

            def add_f(gain):
                r = rstd()
                for k in range(KC):
                    t = tt[:, k % 2, :]
                    own(dve.scalar_tensor_tensor(t, fo[:, k, :], gain(k), r, ALU.mult, ALU.mult))
                    give(dve.tensor_tensor(hc[:, k, 0:SEQ], hc[:, k, 0:SEQ], t, ALU.add), h_ready, "h")

            def norm_gain(layer, i):
                return lambda k: col("norm", (layer * 6 + i) * KC + k)

            def down_loop(first, with_ada=False):
                n0 = c.take("tile", KC)
                with dve.Fori(0, KC // 4) as i:
                    for j in range(4):
                        n = n0 + j
                        dst = fo[:, bass.ds(i * 4 + j, 1), :].rearrange("p a t -> p (a t)")
                        src = ps[:, n % 4, :]
                        dve.wait_ge(tile_done, i * 4 + (n + 1))
                        if first:
                            dve.tensor_copy(dst, src).then_inc(taken, 1)
                        else:
                            dve.tensor_tensor(dst, dst, src, ALU.add).then_inc(taken, 1)
                    if with_ada:
                        g = c.at("ada group")
                        rows = ada_rows[:, bass.ds(i * FOUR + g % 4 * FOUR, FOUR)]
                        dve.wait_ge(ada_done, i * 4 + 4 * (g + 1))
                        dve.tensor_copy(rows, ps[0:2, 6, :]).then_inc(ada_taken, 1)
                if with_ada:
                    c.take("ada group", KC // 4)
                dve.wait_ge(taken, n0 + KC + 4)

            def ffn_phase(layer, i):
                x_from_h(norm_gain(layer, 4 * i))
                for number, part in enumerate(FF_PARTS):
                    n0 = c.take("tile", 2 * part)
                    s0, o0, a0 = c.take("sil", part), c.take("own", part), c.take("a", part)
                    with dve.Fori(0, part // 2) as it:
                        for j in range(2):
                            hi = ah[:, bass.ds(it * (2 * SEQ) + j * SEQ, SEQ)]
                            lo = al[:, bass.ds(it * (2 * SEQ) + j * SEQ, SEQ)]
                            dve.wait_ge(sil_ready, it * 2 + (s0 + j + 1))
                            dve.wait_ge(tile_done, it * 4 + (n0 + 2 * j + 2))
                            dve.tensor_tensor(tt[:, j, :], sil[:, j, :], ps[:, (n0 + 2 * j + 1) % 4, :], ALU.mult).then_inc(taken, 2)
                            dve.wait_ge(taken, it * 4 + (n0 + 2 * j + 6))
                            dve.tensor_copy(hi, tt[:, j, :]).then_inc(dve_own, 1)
                            dve.wait_ge(dve_own, it * 2 + (o0 + j + 1))
                            dve.tensor_tensor(lo, tt[:, j, :], hi.bitcast(F32), ALU.subtract).then_inc(a_ready, 1)
                    dve.wait_ge(a_ready, a0 + part)
                    if number < len(FF_PARTS) - 1:
                        down_loop(number == 0, has_ada(layer, i))
                for m in range(KC):
                    n = tile()
                    took(dve.tensor_tensor(fo[:, m, :], fo[:, m, :], ps[:, n % 4, :], ALU.add), n)
                if (layer, i) == (1, 0):
                    dve.wait_ge(h0_out, 16)
                add_f(norm_gain(layer, 4 * i + 1))
                if has_ada(layer, i):
                    get(p2d, "p2d")
                    m = 4 * (c.at("ada group") - 4)
                    own(dve.tensor_tensor(ada_all[:, m:m + 16, :], ps[:, 7, 0:32].rearrange("p (m s) -> p m s", s=2),
                                          col("bada", m, 16).unsqueeze(2).to_broadcast([P, 16, 2]), ALU.add))

            def pool():
                x_from_h(norm_gain(0, 2))
                own(dve.memset(pads[:, :, 0:PAD], 0.0))
                for m in range(KC):
                    n = tile()
                    w = POOL_WINDOWS[m // 2]
                    took(dve.tensor_copy(pads[:, 0, PAD:], ps[:, n % 4, :]), n)
                    step, src = 1, 0
                    while step < w:
                        dst = 1 if src != 1 else 2
                        own(dve.tensor_tensor(pads[:, dst, PAD:], pads[:, src, PAD:], pads[:, src, PAD - step:PAD + SEQ - step], ALU.add))
                        src, step = dst, 2 * step
                    t = tt[:, 0, :]
                    own(dve.scalar_tensor_tensor(t[:, PAD:], pads[:, src, 2 * PAD:], 1.0 / w, pads[:, 0, 2 * PAD:], ALU.mult, ALU.subtract))
                    cnt = const("cnt")[:, (m // 2) * PAD:(m // 2 + 1) * PAD]
                    own(dve.tensor_tensor(t[:, 0:PAD], pads[:, src, PAD:2 * PAD], cnt, ALU.mult))
                    own(dve.tensor_tensor(t[:, 0:PAD], t[:, 0:PAD], pads[:, 0, PAD:2 * PAD], ALU.subtract))
                    split(t, ahk(m), alk(m), a_ready, "a")
                for g2 in range(2):
                    n = tile()
                    for b in range(4):
                        m = g2 * 4 + b
                        t = tt[:, b % 2, :]
                        ins = dve.tensor_scalar(t, ps[:, b, :], col("pscale", m), None, ALU.mult)
                        took(ins, n) if b == 3 else own(ins)
                        split(t, xh[:, m, 0:SEQ], xl[:, m, 0:SEQ], x_ready, "x")
                down_loop(True)
                add_f(norm_gain(0, 3))

            def divide_round(t, u, v):
                own(dve.tensor_scalar(u, t, MAGIC, None, ALU.add))
                own(dve.tensor_scalar(v, u, MAGIC, None, ALU.subtract))

            def rope_tables():
                get_pos = t1[:, 1, :].bitcast(I32)
                dve.wait_ge(cond_in, 32)
                ang, u, v = tt[:, 0, :], tt[:, 1, :], sq[:, 0, :]
                own(dve.tensor_copy(sq[:, 1, :], get_pos))
                own(dve.tensor_scalar(ang, sq[:, 1, :], const("invf"), None, ALU.mult))
                for s in range(2):
                    own(dve.tensor_scalar(u, ang, 1.0 / (2 * math.pi), 0.25 if s == 0 else 0.0, ALU.mult, ALU.add))
                    divide_round(u, v, u)
                    own(dve.scalar_tensor_tensor(v, u, -C1, ang, ALU.mult, ALU.add))
                    own(dve.scalar_tensor_tensor(v, u, -C2, v, ALU.mult, ALU.add))
                    own(dve.scalar_tensor_tensor(v, u, -C3, v, ALU.mult, ALU.add))
                    if s == 0:
                        own(dve.tensor_scalar(v, v, math.pi / 2, None, ALU.add))
                    else:
                        get(a2d, "a2d")
                    give(dve.tensor_scalar(t1[:, 0, :], v, PI_IN, -PI_IN, ALU.min, ALU.max), d2a, "d2a")
                get(a2d, "a2d")

            def rope(dst, bank, cos, sin, a, b):
                dve.tensor_tensor(a, dst, cos, ALU.mult)
                own(dve.tensor_tensor(b, bank, sin, ALU.mult))
                own(dve.tensor_tensor(dst, a, b, ALU.add))

            def attend(kind, scale, sink=None, minus=None, layer=0):
                units = attention(kind, layer)
                q, k, v, p, pt, o = buffers(kind)
                u0 = c.at("unit")
                g_at = [c.at("group")]

                def maximum(i):
                    n = len(units[i]["blocks"]) * P
                    z = i % 2
                    dve.wait_ge(s_full, u0 + i + 1)
                    own(dve.tensor_reduce(mx[:, z:z + 1], slot(i, units[i]), AX.X, ALU.max))
                    if sink is None:
                        ins = dve.tensor_scalar(negm[:, z:z + 1], mx[:, z:z + 1], -scale, None, ALU.mult)
                    else:
                        own(dve.tensor_scalar(mx[:, z:z + 1], mx[:, z:z + 1], scale, sink(units[i]), ALU.mult, ALU.max))
                        ins = dve.tensor_scalar(negm[:, z:z + 1], mx[:, z:z + 1], -1.0, None, ALU.mult)
                    give(ins, neg_ready, "neg")

                def evacuate(i):
                    for b, blocks in enumerate(groups(units[i])):
                        g = c.take("group")
                        if b % 2:
                            dve.wait_ge(pt_full, g + 1)
                            if i >= 2:
                                dve.wait_ge(o_full, u0 + i - 1)
                            n = len(blocks) * P
                            give(dve.tensor_copy(pt[i % 2][:, blocks[0] * P:blocks[0] * P + n], ps[:, g % 2, 0:n]), pt_dve, "pt_dve")

                def output(i):
                    u, z, y = units[i], i % 2, i % 3
                    dve.wait_ge(p_ready, u0 + i + 1)
                    if sink is not None:
                        own(dve.tensor_tensor(den[:, y:y + 1], den[:, y:y + 1], esink[:, y:y + 1], ALU.add))
                    own(dve.reciprocal(rden[:, z:z + 1], den[:, y:y + 1]))
                    dst = o[:, u["i"] * P + HEAD * u["h"]:u["i"] * P + HEAD * (u["h"] + 1)]
                    if u["add"]:
                        own(dve.tensor_scalar(rden[:, z:z + 1], rden[:, z:z + 1], minus, None, ALU.mult))
                    dve.wait_ge(o_full, u0 + i + 1)
                    if u["add"]:
                        ins = dve.scalar_tensor_tensor(dst, o_psum(i, kind), rden[:, z:z + 1], dst, ALU.mult, ALU.add)
                    else:
                        ins = dve.tensor_scalar(dst, o_psum(i, kind), rden[:, z:z + 1], None, ALU.mult)
                    give(ins, o_taken, "o_taken")

                maximum(0)
                for i in range(len(units)):
                    if i >= 1:
                        evacuate(i - 1)
                    if i + 1 < len(units):
                        maximum(i + 1)
                    if i >= 1:
                        output(i - 1)
                evacuate(len(units) - 1)
                output(len(units) - 1)
                c.take("unit", len(units))

            def dilated():
                x_from_h(norm_gain(1, 2))
                dve.wait_ge(x_ready, c.at("x"))
                rope_tables()
                to_parts(kv_parts(), a_ready, "a", normalised(lambda k: fo[:, k, :], lambda k: col("kv", k)))
                for hp in range(A_HEADS // 2):
                    for g in range(3):
                        for what in range(3):
                            n = tile()
                            took(dve.tensor_copy(fv1 if what == 2 else qk1[:, 2 * g + what, :], ps[:, n % 4, :]), n)
                            if what == 0 and g:
                                values_turned(v1[:, g - 1, :], 5, SEQ)
                            if what == 2:
                                signal(d2p, "d2p")
                            if what:
                                get(p2d, "p2d")
                                last = qk1[:, 2 * g + what - 1, :]
                                rope(last, ps[:, 6 + c.take("rot") % 2, :], cs1[:, 0, :], cs1[:, 1, :], t1[:, 0, :], t1[:, 1, :])
                    values_turned(v1[:, 2, :], 5, SEQ)
                    signal(d2p, "d2p")
                    attend("dilated", HEAD ** -0.5)
                    signal(d2p, "d2p")
                    get(p2d, "p2d")
                    split(ps[:, 4, :], ahk(KC + hp), alk(KC + hp), a_ready, "a")
                for m in range(0, KC, 2):
                    n = tile()
                    b = 2 * (n % 2)
                    took(dve.tensor_copy(fo[:, m:m + 2, :], ps[:, b:b + 2, :]), n)
                add_f(norm_gain(1, 3))

            def ada_phase(layer):
                if layer == 0:
                    own(dve.tensor_scalar(ada[:, :, KC:2 * KC, :], ada[:, :, KC:2 * KC, :], 1.0, None, ALU.add))
                    dve.wait_ge(cond_in, 48)

                def modulated(k, t):
                    for s, (at, w) in enumerate(((0, SEQ), (SEQ, CTX))):
                        ins = dve.tensor_scalar(t[:, at:at + w], hc[:, k, at:at + w], ada[:, layer, KC + k, s:s + 1], ada[:, layer, k, s:s + 1], ALU.mult, ALU.add)
                    return ins

                to_parts(x_parts(layer), x_ready, "x", modulated)
                if layer == 0:
                    own(dve.tensor_tensor(lt[:, 0:4], col("lb", 4, 4), col("lb", 0, 4), ALU.subtract))
                    give(dve.scalar_tensor_tensor(lt[:, 8:12], lt[:, 0:4], -1.0, lt[:, 0:4], ALU.mult, ALU.max), d2a, "d2a")
                    get(a2d, "a2d")
                    own(dve.tensor_scalar(lt[:, 4:8], lt[:, 0:4], -1.0, 0.0, ALU.mult, ALU.min))
                    own(dve.tensor_scalar(lt[:, 0:4], lt[:, 0:4], 0.0, None, ALU.min))
                    own(dve.tensor_tensor(lnlb, lt[:, 0:4], lt[:, 8:12], ALU.subtract))
                    own(dve.tensor_tensor(ln1lb, lt[:, 4:8], lt[:, 8:12], ALU.subtract))
                    for l in range(DEPTH):
                        for a in range(2):
                            one = col("dfl", (l * 4 + 2 * a) * 32, 32)
                            own(dve.tensor_tensor(one, one, col("dfl", (l * 4 + 2 * a + 1) * 32, 32), ALU.mult))
                            own(dve.tensor_reduce(lt[:, 16 + 2 * l + a:17 + 2 * l + a], one, AX.X, ALU.add))
                    signal(d2a, "d2a")
                    get(a2d, "a2d")
                    for l in range(DEPTH):
                        lam_init = 0.8 - 0.6 * math.exp(-0.3 * l)
                        own(dve.tensor_tensor(lamc[:, l:l + 1], lt[:, 17 + 2 * l:18 + 2 * l], lt[:, 16 + 2 * l:17 + 2 * l], ALU.subtract))
                        own(dve.tensor_scalar(lamc[:, l:l + 1], lamc[:, l:l + 1], -lam_init, None, ALU.add))
                        own(dve.tensor_scalar(col("dfg", l), col("dfg", l), 1.0 - lam_init, None, ALU.mult))

            def take_wide(dst, n_tok=TOK):
                n = tile()
                took(dve.tensor_copy(in_runs(dst, n_tok), banks(2 * (n % 2), n_tok)), n)

            def values_turned(dst, b, n):
                get(p2d, "p2d")
                own(dve.tensor_copy(in_runs(dst, n), banks(b, n)))

            def finish(layer, gates, gain, chunk):
                get(p2d, "p2d")
                n = out_tiles(layer) * P
                t = area(3 * TOK, TOK)
                if gain is None:
                    own(dve.tensor_tensor(in_runs(t, n), banks(6, n), in_runs(gates, n), ALU.mult))
                else:
                    own(dve.scalar_tensor_tensor(in_runs(t, n), banks(6, n), gain, in_runs(gates, n), ALU.mult, ALU.mult))
                split(t[:, 0:n], ahk(chunk, TOK)[:, 0:n], alk(chunk, TOK)[:, 0:n], a_ready, "a")

            def head_rms(layer, o, t):
                n, heads = out_tiles(layer) * P, 2 * out_tiles(layer)
                o3, t3 = (z[:, 0:n].rearrange("p (h d) -> p h d", d=HEAD) for z in (o, t))
                own(dve.tensor_tensor(t3, o3, o3, ALU.mult))
                give(dve.tensor_reduce(hs_of(layer), t3, AX.X, ALU.add), d2a, "d2a")
                get(a2d, "a2d")
                give(dve.tensor_tensor(o3, o3, hs_of(layer).unsqueeze(2).to_broadcast([P, heads, HEAD]), ALU.mult), d2p, "d2p")

            def log_forget(z, out_):
                give(dve.scalar_tensor_tensor(se, z, -1.0, z, ALU.mult, ALU.max), d2a, "d2a")
                get(a2d, "a2d")
                own(dve.scalar_tensor_tensor(out_, z, 0.0, se, ALU.min, ALU.subtract))

            def operands(s, t, way, full):
                dve.wait_ge(decay_ready, s + 1)
                b = slice(t * P, (t + 1) * P)
                last = P - 1 if way == 0 else 0
                own(dve.tensor_copy(sd[:, s % 4:s % 4 + 1], qi[s % 3][:, last:last + 1]))
                if full:
                    dve.tensor_tensor(qi[s % 3], qi[s % 3], sq_q[:, b], ALU.mult)
                    for l in range(LEVELS):
                        w = halves(level(s, l), l)
                        k_, q_ = halves(sk[:, b], l)[way], halves(sq_q[:, b], l)[1 - way]
                        dve.tensor_tensor(w[way], w[way], k_, ALU.mult)
                        dve.tensor_tensor(w[1 - way], w[1 - way], q_, ALU.mult)
                dve.tensor_tensor(kd[s % 2], kd[s % 2], sk[:, b], ALU.mult).then_inc(ops_ready, 1)

            def take_products(s, way, full):
                if full:
                    n = c.take("full")
                    dve.wait_ge(near_full, n + 1)
                    if n >= 2:
                        dve.wait_ge(step_full, s - 1)
                    for h in range(2):
                        pv = ps[:, 4 + h, 0:NLOW * BLK].rearrange("p (l t) -> p l t", l=NLOW)
                        ins = dve.tensor_tensor(lowp[:, h], pv, lev[:, way], ALU.mult)
                    own(ins)
                    own(dve.tensor_reduce(lows, lowp.rearrange("p h l t -> p h t l"), AX.X, ALU.add))
                    for h in range(2):
                        ins = dve.tensor_tensor(near[n % 2][:, h, :].rearrange("p (b t) -> p b t", b=P // BLK),
                                                lows[:, h, :].unsqueeze(1).to_broadcast([P, P // BLK, BLK]),
                                                mask("blk32").rearrange("p (b t) -> p b t", b=P // BLK), ALU.mult)
                    ins.then_inc(near_ready, 1)
                dve.wait_ge(turned, s + 1)
                if s >= 2:
                    dve.wait_ge(step_full, s - 1)
                dve.tensor_copy(kdt[s % 2], ps[:, 2, 0:P]).then_inc(kdt_ready, 1)

            def take_step(s, t, way, full):
                dve.wait_ge(step_full, s + 1)
                if full:
                    n = c.take("stepped")
                    dst = so[:, t * P:(t + 1) * P]
                    if way == 0:
                        dve.tensor_copy(dst, ps[:, n % 2, 0:P])
                    else:
                        dve.tensor_tensor(dst, dst, ps[:, n % 2, 0:P], ALU.add)
                for h in range(2):
                    r = slice(HEAD * h, HEAD * (h + 1))
                    sh = state[r, h * HEAD:(h + 1) * HEAD]
                    ins = dve.scalar_tensor_tensor(sh, sh, sd[r, s % 4:s % 4 + 1], ps[r, 3, h * HEAD:(h + 1) * HEAD], ALU.mult, ALU.add)
                ins.then_inc(state_ready, 1)
                dve.wait_ge(state_ready, c.take("state") + 1)

            def running_sums(layer, hp, way):
                if way:
                    own(dve.tensor_copy(sz, sz2))
                log_forget(sz, sw)
                give(dve.tensor_tensor(sk, sw, sz, ALU.subtract), d2a, "d2a")
                get(a2d, "a2d")
                if layer:
                    own(dve.tensor_scalar(sz, sz, lnlb[:, way * 2 + hp:way * 2 + hp + 1], None, ALU.subtract))
                    log_forget(sz, sz)
                    own(dve.tensor_tensor(sz, sw, sz, ALU.subtract))
                else:
                    own(dve.tensor_copy(sz, sw))
                for t in range(NQ):
                    b = slice(t * P, (t + 1) * P)
                    ins = dve.tensor_tensor_scan(sw[:, b], ones, sz[:, b], 0.0, ALU.mult, ALU.add)
                own(ins)
                if way == 0:
                    own(dve.tensor_copy(sz, sw))
                else:
                    own(dve.tensor_tensor(sz, sz, sw, ALU.subtract))
                    for t in range(NQ):
                        b = slice(t * P, (t + 1) * P)
                        ins = dve.tensor_scalar(sz[:, b], sz[:, b], sw[:, (t + 1) * P - 1:(t + 1) * P], None, ALU.add)
                    own(ins)

            def scan(layer, hp):
                for j, (what, dst) in enumerate(zip("qgfif", (sq_q, sg, sz, so, sz2))):
                    take_wide(dst, tokens(what, layer))
                    if j == 2:
                        get(a2d, "a2d", 2)
                        running_sums(layer, hp, 0)
                    if j == 3:
                        signal(d2p, "d2p")
                    if j == 4:
                        values_turned(sv, 6, TOK)
                for way in range(2):
                    if way:
                        running_sums(layer, hp, 1)
                    for f in far:
                        own(dve.memset(f, 0.0))
                    dve.memset(state, 0.0).then_inc(state_ready, 1)
                    dve.wait_ge(state_ready, c.take("state") + 1)
                    dve.sem_inc(sums_ready, 1)
                    s0 = c.take("scan tile", NQ)
                    tiles_ = order(way)
                    for i in range(-1, NQ + 1):
                        if i + 1 < NQ:
                            operands(s0 + i + 1, tiles_[i + 1], way, has_output(tiles_[i + 1], layer))
                        if 0 <= i < NQ:
                            take_products(s0 + i, way, has_output(tiles_[i], layer))
                        if i >= 1:
                            take_step(s0 + i - 1, tiles_[i - 1], way, has_output(tiles_[i - 1], layer))
                head_rms(layer, so, sw)
                finish(layer, sg, col("hgn", layer), hp)

            def attend_phase(layer, kind, hp):
                before = None
                for what in pass_tiles(kind, hp):
                    dst = dict(q=q2, k=k2, v=fv2, g=sg2)[what]
                    n_tok = tokens(what, layer)
                    take_wide(dst, n_tok)
                    if before == "v":
                        values_turned(v2, 6, TOK)
                    before = what
                    if what == "v":
                        signal(d2p, "d2p")
                    if what in "qk":
                        if kind == "global":
                            signal(d2a, "d2a")
                            get(a2d, "a2d")
                            dv = in_runs(dst, n_tok)
                            own(dve.scalar_tensor_tensor(dv, dv, col("gaq" if what == "q" else "gak", layer), banks(6, n_tok), ALU.mult, ALU.mult))
                        signal(d2p, "d2p")
                        get(p2d, "p2d")
                        z = 2 * SEQ if kind == "diff" else 0
                        rope(dst[:, 0:SEQ], ps[:, 5, :], tb[:, z:z + SEQ], tb[:, z + SEQ:z + 2 * SEQ], ta, tbuf)
                        hi, lo = qk_parts(kind, hp)[0 if what == "q" else 2:][:2]
                        own(dve.tensor_copy(hi[:, 0:n_tok], dst[:, 0:n_tok]))
                        own(dve.tensor_tensor(lo[:, 0:n_tok], dst[:, 0:n_tok], hi[:, 0:n_tok].bitcast(F32), ALU.subtract))
                get(a2d, "a2d")
                signal(d2p, "d2p")
                if kind == "window":
                    attend(kind, HEAD ** -0.5, lambda u: col("sink", layer * 4 + 2 * u["h"] + hp), layer=layer)
                else:
                    attend(kind, (HEAD // 2 if kind == "diff" else HEAD) ** -0.5, minus=lamc[:, layer:layer + 1], layer=layer)
                if kind == "diff":
                    head_rms(layer, o2, area(3 * TOK, TOK))
                else:
                    signal(d2p, "d2p")
                finish(layer, sg2, col("dfg", layer) if kind == "diff" else None, 2 * ["scan", "global", "diff", "window"].index(kind) + hp)

            def mix(layer):
                n = out_tiles(layer) * P
                for m in range(KC):
                    t = area((4 + m % 2) * TOK, TOK)
                    take_wide(t, n)
                    for s, (at, w) in enumerate(((0, SEQ), (SEQ, n - SEQ))):
                        if w:
                            ins = dve.tensor_scalar(t[:, at:at + w], t[:, at:at + w], ada[:, layer, 2 * KC + m, s:s + 1], None, ALU.mult)
                    own(ins)
                    give(dve.scalar_tensor_tensor(hc[:, m, 0:n], hc[:, m, 0:n], ALPHA, t[:, 0:n], ALU.mult, ALU.add), d2p, "d2p")
                get(p2d, "p2d")
                for k in range(KC):
                    hv = in_runs(hc[:, k, :], n)
                    c.take("d2a")
                    dve.scalar_tensor_tensor(hv, banks(4, n), -1.0 / D, hv, ALU.mult, ALU.add).then_inc(d2a, 1)
                dve.wait_ge(d2a, c.at("d2a"))
                get(a2d, "a2d")
                for k in range(KC):
                    hv = in_runs(hc[:, k, :], n)
                    own(dve.scalar_tensor_tensor(hv, hv, col("lng", layer * KC + k), banks(6, n), ALU.mult, ALU.mult))
                    give(dve.tensor_scalar(hc[:, k, 0:n], hc[:, k, 0:n], col("lnb", layer * KC + k), None, ALU.add), h_ready, "h")

            dve.wait_ge(const_in, CONST_LOADS * 16)
            own(dve.tensor_copy(mk[:, :], area(0, NMASK)))
            own(dve.tensor_copy(lev.rearrange("p a l t -> p (a l t)"), area(NMASK, NLEV)))
            own(dve.memset(eps_c, EPS))
            own(dve.memset(ln_eps_c, LN_EPS))
            own(dve.memset(one_c, 1.0))
            for layer in range(DEPTH):
                for i in (1, 5):
                    g = col("norm", (layer * 6 + i) * KC, KC)
                    own(dve.tensor_scalar(g, g, 0.5, None, ALU.mult))
            dve.sem_inc(ada_taken, 1)
            dve.sem_inc(taken, 4)
            dve.sem_inc(h_ready, KC)
            c.take("h", KC)
            run = dict(ffn=ffn_phase, pool=pool, keep=lambda: None, dilated=dilated, ada=ada_phase, scan=scan, attend=attend_phase, mix=mix)
            for name, *rest in PHASES:
                run[name](*rest)


_PROGRAM_INPUTS = ("wts", "par", "con", "tab", "masks", "levels", "pos", "x", "ctx")


def lay_out(inputs):
    a = {k: np.asarray(v) for k, v in inputs.items()}
    con, masks, levels = constants()
    return {
        "wts": lay_out_tiles(a),
        "par": np.ascontiguousarray(lay_out_parameters(a)),
        "con": np.ascontiguousarray(con[:, :NCON]),
        "tab": np.ascontiguousarray(con[:, NCON:]),
        "masks": masks.astype(np.float32),
        "levels": levels,
        "pos": np.ascontiguousarray(np.broadcast_to(a["positions"], (P, SEQ))),
        "x": np.ascontiguousarray(a["x"][0].T),
        "ctx": np.ascontiguousarray(a["ctx_2"][0].T.reshape(KC, P, CTX).transpose(1, 0, 2)),
    }


def program(nc, arrays, stop=None):
    args = []
    for name in _PROGRAM_INPUTS:
        v = arrays[name]
        args.append(nc.dram_tensor(name + "_dram", v.shape, mybir.dt.from_np(v.dtype), kind="ExternalInput").ap())
    out = nc.dram_tensor("out_dram", (D, SEQ), F32, kind="ExternalOutput").ap()
    scratch = nc.dram_tensor("kept_dram", (P, KC, SEQ), F32, kind="Internal").ap()
    build(nc, *args, out, scratch, stop=stop)


def kernel(**inputs):
    import concourse.bacc as bacc
    from concourse.bass_utils import run_bass_kernel_spmd

    nc = bacc.Bacc("TRN2", target_bir_lowering=False, num_devices=1)
    arrays = lay_out(inputs)
    program(nc, arrays)
    r = run_bass_kernel_spmd(nc, [{k + "_dram": v for k, v in arrays.items()}], core_ids=[0])
    return np.ascontiguousarray(r.results[0]["out_dram"].T)[None]
```
